# Optimizing a Trainium2 kernel written in Bass

```python
import math
import jax, jax.numpy as jnp
from jax import lax
import numpy as np

D_MODEL = 1024
BATCH = 1
SEQ = 512
DEPTH = 2

N_META = 16
EPS = 1e-6
NEG_INF = -1e30
N_A_LAYERS = DEPTH // 2
N_B_LAYERS = DEPTH - N_A_LAYERS
SSM_EXPAND = 2
D_INNER = SSM_EXPAND * D_MODEL
SSM_HEADDIM = 64
SSM_HEADS = D_INNER // SSM_HEADDIM
SSM_GROUPS = 8
SSM_HPG = SSM_HEADS // SSM_GROUPS
SSM_STATE = 128
SSM_CONV = 4
SSM_CHUNK = 256
CONV_DIM = D_INNER + 2 * SSM_GROUPS * SSM_STATE
IN_PROJ_DIM = D_INNER + CONV_DIM + SSM_HEADS
DIFF_HEADS = 8
DIFF_HEAD_DIM = D_MODEL // DIFF_HEADS // 2
DIFF_VDIM = 2 * DIFF_HEAD_DIM
Q_BLOCK = 128
REL_BUCKETS = 32
REL_MAX_DIST = 128
FFN_HIDDEN = (((8 * D_MODEL + 2) // 3) + 255) // 256 * 256

kernel_name = "yoco_mamba2_diffattn_hybrid"

def _rmsnorm(x, w):
    xf = x.astype(jnp.float32)
    y = xf * lax.rsqrt(jnp.mean(xf * xf, axis=-1, keepdims=True) + EPS)
    return (y * w.astype(jnp.float32)).astype(x.dtype)

def _swiglu(u, w_gu, w_down):
    g, v = jnp.split(u @ w_gu, 2, axis=-1)
    return (jax.nn.silu(g) * v) @ w_down

def _causal_dwconv(xbc, w, b):
    c = xbc.shape[-1]
    out = lax.conv_general_dilated(
        xbc, w[:, None, :], window_strides=(1,), padding=[(SSM_CONV - 1, 0)],
        dimension_numbers=("NWC", "WIO", "NWC"), feature_group_count=c)
    return out + b

def _ssd_mixer(u, in_w, conv_w, conv_b, dt_bias, a_log, d_skip, norm_w, out_w):
    bsz, L, _ = u.shape
    zxbcdt = u @ in_w
    z = zxbcdt[..., :D_INNER]
    xbc = zxbcdt[..., D_INNER:D_INNER + CONV_DIM]
    dt_raw = zxbcdt[..., D_INNER + CONV_DIM:]
    xbc = jax.nn.silu(_causal_dwconv(xbc, conv_w, conv_b))
    dt = jax.nn.softplus(dt_raw.astype(jnp.float32) + dt_bias.astype(jnp.float32))

    n_real = L - N_META
    pad_l = SSM_CHUNK - N_META
    pad_r = (-n_real) % SSM_CHUNK
    xbc_p = jnp.pad(xbc.astype(jnp.float32), ((0, 0), (pad_l, pad_r), (0, 0)))
    dt_p = jnp.pad(dt, ((0, 0), (pad_l, pad_r), (0, 0)))
    T = L + pad_l + pad_r
    nc = T // SSM_CHUNK
    G, R, P, N, Q = SSM_GROUPS, SSM_HPG, SSM_HEADDIM, SSM_STATE, SSM_CHUNK
    xs = xbc_p[..., :D_INNER].reshape(bsz, nc, Q, G, R, P)
    Bm = xbc_p[..., D_INNER:D_INNER + G * N].reshape(bsz, nc, Q, G, N)
    Cm = xbc_p[..., D_INNER + G * N:].reshape(bsz, nc, Q, G, N)
    dtc = dt_p.reshape(bsz, nc, Q, G, R)
    A = -jnp.exp(a_log.astype(jnp.float32)).reshape(G, R)
    dA = dtc * A
    to_front = lambda t: jnp.moveaxis(t, 1, 0)
    causal = jnp.tril(jnp.ones((Q, Q), dtype=bool))[None, :, :, None, None]

    def chunk_step(h, inp):
        xc, bc, cc, dtk, dak = inp
        acs = jnp.cumsum(dak, axis=1)
        seg = acs[:, :, None] - acs[:, None, :]
        decay = jnp.exp(jnp.where(causal, seg, NEG_INF))
        cb = jnp.einsum("blgn,bsgn->blsg", cc, bc)
        wts = cb[..., None] * decay * dtk[:, None]
        y_diag = jnp.einsum("blsgr,bsgrp->blgrp", wts, xc)
        y_off = jnp.einsum("blgn,bgrpn->blgrp", cc, h) * jnp.exp(acs)[..., None]
        a_last = acs[:, -1]
        wstate = jnp.exp(a_last[:, None] - acs) * dtk
        h_new = h * jnp.exp(a_last)[..., None, None] + jnp.einsum(
            "bsgn,bsgr,bsgrp->bgrpn", bc, wstate, xc)
        return h_new, y_diag + y_off

    h0 = jnp.zeros((bsz, G, R, P, N), jnp.float32)
    _, ys = lax.scan(chunk_step, h0, (to_front(xs), to_front(Bm), to_front(Cm),
                                      to_front(dtc), to_front(dA)))
    y = jnp.moveaxis(ys, 0, 1).reshape(bsz, T, SSM_HEADS, P)[:, pad_l:pad_l + L]
    x_heads = xbc[..., :D_INNER].astype(jnp.float32).reshape(bsz, L, SSM_HEADS, P)
    y = y + x_heads * d_skip.astype(jnp.float32)[:, None]
    y = y.reshape(bsz, L, D_INNER) * jax.nn.silu(z.astype(jnp.float32))
    yg = y.reshape(bsz, L, G, D_INNER // G)
    yg = yg * lax.rsqrt(jnp.mean(yg * yg, axis=-1, keepdims=True) + EPS)
    y = yg.reshape(bsz, L, D_INNER) * norm_w.astype(jnp.float32)
    return y.astype(u.dtype) @ out_w

def _rel_bucket(rel):
    n = jnp.maximum(-rel, 0)
    max_exact = REL_BUCKETS // 2
    nf = jnp.maximum(n, 1).astype(jnp.float32)
    large = max_exact + (jnp.log(nf / max_exact) / math.log(REL_MAX_DIST / max_exact)
                         * (REL_BUCKETS - max_exact)).astype(jnp.int32)
    large = jnp.minimum(large, REL_BUCKETS - 1)
    return jnp.where(n < max_exact, n, large)

def _diff_attention(u, w_q, lam_q1, lam_k1, lam_q2, lam_k2, subln_w, w_o, k, v, rel_table, lambda_init):
    bsz, L, _ = u.shape
    H, dh = DIFF_HEADS, DIFF_HEAD_DIM
    q = (u @ w_q).reshape(bsz, L, H, 2, dh) * (dh ** -0.5)
    f32 = jnp.float32
    lam = (jnp.exp(jnp.sum(lam_q1.astype(f32) * lam_k1.astype(f32)))
           - jnp.exp(jnp.sum(lam_q2.astype(f32) * lam_k2.astype(f32))) + lambda_init)

    pad_l = Q_BLOCK - N_META
    pad_r = (-(L - N_META)) % Q_BLOCK
    padw = lambda t: jnp.pad(t, ((0, 0), (pad_l, pad_r)) + ((0, 0),) * (t.ndim - 2))
    q_p, k_p, v_p = padw(q), padw(k), padw(v)
    Lp = L + pad_l + pad_r
    nb = Lp // Q_BLOCK
    pos = jnp.arange(Lp, dtype=jnp.int32) - pad_l
    kvalid = (pos >= 0) & (pos < L)
    q_blocks = jnp.moveaxis(q_p.reshape(bsz, nb, Q_BLOCK, H, 2, dh), 1, 0)
    qpos_blocks = pos.reshape(nb, Q_BLOCK)

    def one_block(args):
        qb, qpos = args
        logits = jnp.einsum("bqhcd,bkhcd->bhcqk", qb, k_p).astype(f32)
        bias = rel_table.astype(f32)[_rel_bucket(pos[None, :] - qpos[:, None])]
        bias = jnp.transpose(bias, (2, 0, 1))[None, :, None]
        mask = (pos[None, :] <= qpos[:, None]) & kvalid[None, :]
        logits = jnp.where(mask, logits + bias, NEG_INF)
        p = jax.nn.softmax(logits, axis=-1)
        attn = p[:, :, 0] - lam * p[:, :, 1]
        return jnp.einsum("bhqk,bkhe->bqhe", attn, v_p.astype(f32))

    o = lax.map(one_block, (q_blocks, qpos_blocks))
    o = jnp.moveaxis(o, 0, 1).reshape(bsz, Lp, H, DIFF_VDIM)[:, pad_l:pad_l + L]
    o = o * lax.rsqrt(jnp.mean(o * o, axis=-1, keepdims=True) + EPS)
    o = o * subln_w.astype(f32) * (1.0 - lambda_init)
    return o.reshape(bsz, L, D_MODEL).astype(u.dtype) @ w_o

def setup_inputs(seed: int = 0) -> dict:
    key = jax.random.key(seed)
    ks = iter(jax.random.split(key, 32))
    nrm = lambda shape, s: jax.random.normal(next(ks), shape, jnp.float32) * s
    x = nrm((BATCH, SEQ, D_MODEL), 1.0)
    meta_tokens = nrm((N_META, D_MODEL), 1.0)
    norm_w = 1.0 + nrm((DEPTH, 2, D_MODEL), 0.01)
    ssm_in_w = nrm((N_A_LAYERS, D_MODEL, IN_PROJ_DIM), D_MODEL ** -0.5)
    ssm_conv_w = nrm((N_A_LAYERS, SSM_CONV, CONV_DIM), SSM_CONV ** -0.5)
    ssm_conv_b = nrm((N_A_LAYERS, CONV_DIM), 0.02)
    dt0 = jnp.exp(jax.random.uniform(next(ks), (N_A_LAYERS, SSM_HEADS), jnp.float32,
                                     math.log(1e-3), math.log(1e-1)))
    ssm_dt_bias = dt0 + jnp.log(-jnp.expm1(-dt0))
    ssm_a_log = jnp.log(jax.random.uniform(next(ks), (N_A_LAYERS, SSM_HEADS), jnp.float32, 1.0, 16.0))
    ssm_d = 1.0 + nrm((N_A_LAYERS, SSM_HEADS), 0.01)
    ssm_norm_w = 1.0 + nrm((N_A_LAYERS, D_INNER), 0.01)
    ssm_out_w = nrm((N_A_LAYERS, D_INNER, D_MODEL), D_INNER ** -0.5)
    kv_norm_w = 1.0 + nrm((D_MODEL,), 0.01)
    w_kv = nrm((D_MODEL, 2 * D_MODEL), D_MODEL ** -0.5)
    w_q = nrm((N_B_LAYERS, D_MODEL, D_MODEL), D_MODEL ** -0.5)
    lam_q1 = nrm((N_B_LAYERS, DIFF_HEAD_DIM), 0.1)
    lam_k1 = nrm((N_B_LAYERS, DIFF_HEAD_DIM), 0.1)
    lam_q2 = nrm((N_B_LAYERS, DIFF_HEAD_DIM), 0.1)
    lam_k2 = nrm((N_B_LAYERS, DIFF_HEAD_DIM), 0.1)
    subln_w = 1.0 + nrm((N_B_LAYERS, DIFF_VDIM), 0.01)
    w_o = nrm((N_B_LAYERS, D_MODEL, D_MODEL), D_MODEL ** -0.5)
    rel_bias = nrm((REL_BUCKETS, DIFF_HEADS), 0.5)
    ffn_w_gu = nrm((DEPTH, D_MODEL, 2 * FFN_HIDDEN), D_MODEL ** -0.5)
    ffn_w_down = nrm((DEPTH, FFN_HIDDEN, D_MODEL), FFN_HIDDEN ** -0.5)
    final_norm_w = 1.0 + nrm((D_MODEL,), 0.01)
    return {"x": x, "meta_tokens": meta_tokens, "norm_w": norm_w,
            "ssm_in_w": ssm_in_w, "ssm_conv_w": ssm_conv_w, "ssm_conv_b": ssm_conv_b,
            "ssm_dt_bias": ssm_dt_bias, "ssm_a_log": ssm_a_log, "ssm_d": ssm_d,
            "ssm_norm_w": ssm_norm_w, "ssm_out_w": ssm_out_w,
            "kv_norm_w": kv_norm_w, "w_kv": w_kv, "w_q": w_q,
            "lam_q1": lam_q1, "lam_k1": lam_k1, "lam_q2": lam_q2, "lam_k2": lam_k2,
            "subln_w": subln_w, "w_o": w_o, "rel_bias": rel_bias,
            "ffn_w_gu": ffn_w_gu, "ffn_w_down": ffn_w_down, "final_norm_w": final_norm_w}

def reference(x, meta_tokens, norm_w, ssm_in_w, ssm_conv_w, ssm_conv_b, ssm_dt_bias, ssm_a_log,
              ssm_d, ssm_norm_w, ssm_out_w, kv_norm_w, w_kv, w_q, lam_q1, lam_k1, lam_q2, lam_k2,
              subln_w, w_o, rel_bias, ffn_w_gu, ffn_w_down, final_norm_w):
    bsz = x.shape[0]
    meta = jnp.broadcast_to(meta_tokens.astype(x.dtype)[None], (bsz, N_META, D_MODEL))
    h = jnp.concatenate([meta, x], axis=1)
    L = h.shape[1]
    k_shared = None
    v_shared = None
    for layer in range(DEPTH):
        if layer < N_A_LAYERS:
            i = layer
            h = h + _ssd_mixer(_rmsnorm(h, norm_w[layer, 0]), ssm_in_w[i], ssm_conv_w[i],
                               ssm_conv_b[i], ssm_dt_bias[i], ssm_a_log[i], ssm_d[i],
                               ssm_norm_w[i], ssm_out_w[i])
        else:
            if layer == N_A_LAYERS:
                kv = _rmsnorm(h, kv_norm_w) @ w_kv
                k_shared = kv[..., :D_MODEL].reshape(bsz, L, DIFF_HEADS, 2, DIFF_HEAD_DIM)
                v_shared = kv[..., D_MODEL:].reshape(bsz, L, DIFF_HEADS, DIFF_VDIM)
            j = layer - N_A_LAYERS
            lambda_init = 0.8 - 0.6 * math.exp(-0.3 * layer)
            h = h + _diff_attention(_rmsnorm(h, norm_w[layer, 0]), w_q[j], lam_q1[j], lam_k1[j],
                                    lam_q2[j], lam_k2[j], subln_w[j], w_o[j],
                                    k_shared, v_shared, rel_bias, lambda_init)
        h = h + _swiglu(_rmsnorm(h, norm_w[layer, 1]), ffn_w_gu[layer], ffn_w_down[layer])
    h = _rmsnorm(h, final_norm_w)
    return h[:, N_META:]


_drawn_inputs = setup_inputs


def setup_inputs(seed=0):
    import zlib

    import numpy as np

    out = dict(_drawn_inputs(seed))
    spreads = {}
    factors = {'norm_w': 3.532,
     'ssm_d': 64.0,
     'ssm_norm_w': 6.115,
     'kv_norm_w': 8.0,
     'lam_q1': 26.639,
     'subln_w': 64.0,
     'final_norm_w': 33.656}
    for name, (base, spread) in spreads.items():
        noise = np.random.default_rng([zlib.crc32(name.encode()), seed]).standard_normal(out[name].shape)
        drawn = base * np.exp(spread * noise) if base else spread * noise
        out[name] = __import__('jax').numpy.asarray(drawn.astype(out[name].dtype))
    for name, factor in factors.items():
        out[name] = (out[name] * factor).astype(out[name].dtype)
    return out
```

```python
import math
from contextlib import ExitStack

import numpy as np

import concourse.bass as bass
from concourse import mybir

F32 = mybir.dt.float32
F32R = mybir.dt.float32r
ALU = mybir.AluOpType
ACT = mybir.ActivationFunctionType

P = 128
D = 1024
KT = D // P
META, SEQ = 16, 512
T = META + SEQ
H2 = T // 2
G, HPG = 8, 4
HEADS = G * HPG
TAPS = 4
FT = 22
AH = 8
EARLY = 6
EPS = 1e-6
LAMBDA_INIT = 0.8 - 0.6 * math.exp(-0.3 * 1)
BUCKETS, MAX_DIST = 32, 128
CH = [(0, META)] + [(META + P * i, P) for i in range(SEQ // P)]
NC = len(CH)
NR, RW = 6, T // 6
DIST = [T - 1 - m for m in range(T - 1 + P)]
ND = len(DIST)

U_IN, N_IN = 1, 1
U_OUT1, N_OUT1 = U_IN + 6 * G, N_IN + 6 * G
U_OUT2, N_OUT2 = U_OUT1 + KT, N_OUT1 + KT
U_GU0, N_GU0 = U_OUT2 + KT, N_OUT2 + KT
U_DN0, N_DN0 = U_GU0 + 2 * FT, N_GU0 + 2 * FT
U_KVQ, N_KVQ = U_DN0 + 3 * KT, N_DN0 + KT
U_O1, N_O1 = U_KVQ + 3 * AH, N_KVQ + 3 * AH
U_O2, N_O2 = U_O1 + KT, N_O1 + KT
U_GU1, N_GU1 = U_O2 + 2, N_O2 + KT
U_DN1, N_DN1 = U_GU1 + 2 * FT, N_GU1 + 2 * FT
UNITS = U_DN1 + 3 * KT

C_NORM = 0
C_SSMN = C_NORM + 48
C_DSKIP = C_SSMN + 16
C_CONV = C_DSKIP + 16
C_SUBLN = C_CONV + 4 * G * 5
C_DTB = C_SUBLN + 1
C_ALOG = C_DTB + 1
C_LAM = C_ALOG + 1
C_REL = C_LAM + 4
C_EPS = C_REL + AH
C_ZERO = C_EPS + 2
NPAR = C_ZERO + 1
K_ONES, K_ID, K_MASK, K_HOT = 0, P, 2 * P, 3 * P
K_POS = K_HOT + ND
NCON = K_POS + ND

ATANH = [1 / 15, 1 / 13, 1 / 11, 1 / 9, 1 / 7, 1 / 5, 1 / 3]


def later(count):
    return not isinstance(count, int) or count > 0


def at(i, n=1):
    return slice(i, i + n) if isinstance(i, int) else bass.ds(i, n)


def build(nc, w_all, x_t, par_d, con_d, out_d):
    ctx = ExitStack()
    with ctx:
        base = (nc.sbuf_base + 63) // 64 * 64
        top = nc.sbuf_usable_end

        def place(name, shape, dt, off):
            size = 4 * int(np.prod(shape[1:]))
            assert base + off + size <= top, (name, base + off + size - top)
            return nc.alloc_sbuf_tensor_at(name, shape, dt, offset=base + off), off + (size + 31) // 32 * 32

        def sem(name):
            return ctx.enter_context(nc.semaphore(name))

        o = 0
        uh, o = place("uh", [P, KT, T], F32R, o)
        ul, o = place("ul", [P, KT, T], F32R, o)
        raw, wh, wl = [], [], []
        for s in range(3):
            t, o = place(f"raw{s}", [P, KT, P], F32, o)
            raw.append(t)
            t, o = place(f"wh{s}", [P, KT, P], F32R, o)
            wh.append(t)
            t, o = place(f"wl{s}", [P, KT, P], F32R, o)
            wl.append(t)
        ssq, o = place("ssq", [P, T], F32, o)
        sqt, o = place("sqt", [P, 2, T], F32, o)
        rb, o = place("rb", [P, T], F32, o)
        diag, o = place("diag", [RW, NR, RW], F32, o)
        sd, o = place("sd", [RW, 8], F32, o)
        rc, o = place("rc", [RW, 8], F32, o)
        par, o = place("par", [P, NPAR], F32, o)
        con, o = place("con", [P, 3 * P], F32, o)
        lam, o = place("lam", [P, 8], F32, o)
        negA, o = place("negA", [HEADS, 8], F32, o)
        h, o = place("h", [P, KT, T], F32, o)
        oh = o - 4 * KT * T
        phase = o

        ones = con[:, K_ONES:K_ONES + P]
        ident = con[:, K_ID:K_ID + P]
        mask = con[:, K_MASK:K_MASK + P]

        cv, _ = place("cv", [P, 2, 4, T], F32, oh)
        part, _ = place("part", [P, KT, T], F32, 0)
        o = phase
        yh, o = place("yh", [P, 2 * G, T], F32R, o)
        yl0 = o
        yl, o = place("yl", [P, 2 * G, T], F32R, o)
        dt_tmp, _ = place("dt_tmp", [HEADS, 10, T], F32, yl0 + 4 * T * 6)
        cong, _ = place("cong", [BUCKETS, 2 * ND], F32, phase + 4 * T * 6)
        gvec, _ = place("gvec", [AH, ND], F32, phase + 4 * T * 12)
        rawc, o = place("rawc", [P, T + TAPS - 1], F32, o)
        th, o = place("th", [P, T], F32, o)
        zth, o = place("zth", [P, T], F32, o)
        zs, o = place("zs", [P, 2, 2, T], F32, o)
        ybuf, o = place("ybuf", [P, 2, T], F32, o)
        y2, o = place("y2", [P, 2, T], F32, o)
        bc, o = place("bc", [P, 2, 2, HPG, P], F32, o)
        Lm, o = place("Lm", [P, 2, HPG, P], F32, o)
        Cs, o = place("Cs", [P, 2, HPG, P], F32, o)
        xdt, o = place("xdt", [P, 2, HPG * 64], F32, o)
        xst, o = place("xst", [P, 2, HPG * 64], F32, o)
        Btok, o = place("Btok", [P, 2, P], F32, o)
        cbm, o = place("cbm", [P, 2, P], F32, o)
        state, o = place("state", [P, HPG * 64], F32, o)
        stmp, o = place("stmp", [P, HPG * 64], F32, o)
        tok, o = place("tok", [P, NC, 3, HEADS], F32, o)

        decg, o = place("decg", [P, 2, NC, HPG], F32, o)

        o = phase
        hh, o = place("hh", [P, FT, T], F32R, o)
        hl, o = place("hl", [P, FT, T], F32R, o)
        gb, o = place("gb", [P, 3, T], F32, o)
        vb, o = place("vb", [P, 3, T], F32, o)

        o = phase
        kh, o = place("kh", [P, KT, T], F32R, o)
        kl, o = place("kl", [P, KT, T], F32R, o)
        oTh, o = place("oTh", [P, AH, T], F32R, o)
        oTl, o = place("oTl", [P, AH, T], F32R, o)
        kT, o = place("kT", [P, 2, T], F32, o)
        qT, o = place("qT", [P, 2, T], F32, o)
        vT, o = place("vT", [P, T], F32, o)
        vtok, o = place("vtok", [P, NC, P], F32, o)
        bias, o = place("bias", [P, 2, T], F32, o)
        pr, o = place("pr", [P, 2, 2, T], F32, o)
        aT, o = place("aT", [P, 2, NC, P], F32, o)
        oraw, o = place("oraw", [P, 2, T], F32, o)
        on, o = place("on", [P, T], F32, o)
        rb2, o = place("rb2", [P, T], F32, o)
        sm, o = place("sm", [P, 2, 9], F32, o)

        acc = [ctx.enter_context(nc.psum_tensor(f"acc{p}", [P, 2, 512], F32)) for p in range(2)]
        psAY = ctx.enter_context(nc.psum_tensor("psAY", [P, 2, 512], F32))
        psA, psY = psAY[:, 0, :], psAY[:, 1, :]
        psS = ctx.enter_context(nc.psum_tensor("psS", [P, 512], F32))
        psF = ctx.enter_context(nc.psum_tensor("psF", [P, 512], F32))

        scr = nc.dram_tensor("scr_acs", [2, HEADS, T], F32, kind="Internal").ap()
        scr_b = nc.dram_tensor("scr_bias", [AH, P * ND], F32, kind="Internal").ap()

        raw_in = [sem(f"raw_in{s}") for s in range(3)]
        hi_ready = sem("hi_ready")
        lo_ready = sem("lo_ready")
        unit_done = sem("unit_done")
        acc_free = [sem("acc_free0"), sem("acc_free1")]
        x_in, par_in, con_in, cong_in = sem("x_in"), sem("par_in"), sem("con_in"), sem("cong_in")
        x_sem = [sem(f"x_in{q}") for q in range(4)]
        sq_done, ssq_done, ssq_zero = sem("sq_done"), sem("ssq_done"), sem("ssq_zero")
        n_stat, n_sd, n_rc, n_diag = sem("n_stat"), sem("n_sd"), sem("n_rc"), sem("n_diag")
        n_bc, n_rb = sem("n_bc"), sem("n_rb")
        decg_done = sem("decg_done")
        u_f, u_hi, u_lo = sem("u_f"), sem("u_hi"), sem("u_lo")
        setup = sem("setup")
        lam_mm, lam_exp, hot_mm, gvec_out = sem("lam_mm"), sem("lam_exp"), sem("hot_mm"), sem("gvec_out")
        dt_v, dt_a, tok_t, tok_ready, scr_out = (
            sem("dt_v"), sem("dt_a"), sem("tok_t"), sem("tok_ready"), sem("scr_out"))
        raw_copied, tap2_done, tap1_done, taps_done = (
            sem("raw_copied"), sem("tap2_done"), sem("tap1_done"), sem("taps_done"))
        tanh_done, conv_ready, ztanh_done = sem("tanh_done"), sem("conv_ready"), sem("ztanh_done")
        bc_in = [sem("bc_in0"), sem("bc_in1")]
        chunk_t, xdt_done, cbm_done, seg_done, exp_done, wt_done = (
            sem("chunk_t"), sem("xdt_done"), sem("cbm_done"), sem("seg_done"), sem("exp_done"), sem("wt_done"))
        xst_done, cs_done, scan_done, stmp_done, st_done, yadd_done = (
            sem("xst_done"), sem("cs_done"), sem("scan_done"), sem("stmp_done"), sem("st_done"), sem("yadd_done"))
        y2_done, f_sq, f_stat, f_sd, f_rc, f_diag, f_bc, f_rb, f_yn, f_hi, f_lo = (
            sem("y2_done"), sem("f_sq"), sem("f_stat"), sem("f_sd"), sem("f_rc"), sem("f_diag"), sem("f_bc"),
            sem("f_rb"), sem("f_yn"), sem("f_hi"), sem("f_lo"))
        part_in = sem("part_in")
        k_hi, k_lo = sem("k_hi"), sem("k_lo")
        bias_in = [sem("bias_in0"), sem("bias_in1")]
        v_t, v_tok, s_mm, s_max, p_exp, p_rec, p_lam, p_half, p_comb = (
            sem("v_t"), sem("v_tok"), sem("s_mm"), sem("s_max"), sem("p_exp"), sem("p_rec"), sem("p_lam"),
            sem("p_half"), sem("p_comb"))
        p_t, p_tc, o_mm, o_out, o2_mm = sem("p_t"), sem("p_tc"), sem("o_mm"), sem("o_out"), sem("o2_mm")
        h_sq, h_stat, h_sd, h_rc, h_diag, h_bc, h_rb, h_on, h_hi, h_lo = (
            sem("h_sq"), sem("h_stat"), sem("h_sd"), sem("h_rc"), sem("h_diag"), sem("h_bc"), sem("h_rb"),
            sem("h_on"), sem("h_hi"), sem("h_lo"))
        silu_done, hid_done, hid_hi, hid_lo = sem("silu_done"), sem("hid_done"), sem("hid_hi"), sem("hid_lo")
        out_f, stored = sem("out_f"), sem("stored")

        block = ctx.enter_context(nc.Block())

        class Idx:

            def __init__(self, first, rate=0, turn=0):
                self.first, self.rate, self.turn = first, rate, turn

            def __add__(self, k):
                return Idx(self.first + k, self.rate, self.turn)

            def mul(self, k, plus=0):
                return self.turn * (self.rate * k) + (self.first * k + plus) if self.rate else self.first * k + plus

            @property
            def v(self):
                return self.mul(1)

            def times(self, k, plus=0):
                return Idx(self.first * k + plus, self.rate * k, self.turn)

            def div(self, m):
                assert self.rate % m == 0
                return Idx(self.first // m, self.rate // m, self.turn)

        def load_unit(e, u):
            s = u.first % 3
            if later((u + -2).v):
                e.wait_ge(lo_ready, (u + -2).v)
            e.dma_start(raw[s][:].rearrange("p k c -> p (k c)"),
                        w_all[at(u.v)].rearrange("a p f -> p (a f)")).then_inc(raw_in[s], 16)

        def split_hi(e, u):
            s = u.first % 3
            e.wait_ge(raw_in[s], u.div(3).mul(16, 16))
            if later((u + -2).v):
                e.wait_ge(unit_done, (u + -2).v)
            e.activation(wh[s][:], raw[s][:], ACT.Copy).then_inc(hi_ready, 1)

        def split_lo(e, u):
            s = u.first % 3
            e.wait_ge(hi_ready, (u + 1).v)
            e.tensor_tensor(wl[s][:], raw[s][:], wh[s][:].bitcast(F32), ALU.subtract).then_inc(lo_ready, 1)

        def look_ahead(e, split, u):
            if u.rate or u.first + 3 < UNITS:
                split(e, u + 3)

        def multiply(e, u, n, xh, xl, k0=0, ks=KT, first=True, last=True, slices=None, moving=None):
            s, a = u.first % 3, acc[n.first % 2]
            for k in (range(ks) if slices is None else slices):
                if k == 0:
                    e.wait_ge(lo_ready, (u + 1).v)
                    if first:
                        if later(n.div(2).v):
                            e.wait_ge(acc_free[n.first % 2], n.div(2).v)
                if moving:
                    e.wait_ge(moving[0], moving[1] + k + 1)
                for i, (wt, mv) in enumerate(((wh, xh), (wh, xl), (wl, xh))):
                    for half in range(2):
                        mm = e.matmul(a[:, half, 0:H2], wt[s][:, k, :], mv[:, k0 + k, H2 * half:H2 * half + H2],
                                      start=(first and k == 0 and i == 0), stop=(last and k == ks - 1 and i == 2))
                if k == ks - 1:
                    mm.then_inc(unit_done, 1)

        def halves(t):
            return t.rearrange("p (a b) -> p a b", a=2)

        def taken(e, n):
            e.wait_ge(acc_free[n.first % 2], n.div(2).mul(1, 1))

        def acc_of(n):
            return acc[n.first % 2][:, :, 0:H2]

        def free(ins, n):
            ins.then_inc(acc_free[n.first % 2], 1)

        def stats(e, src, n_src, at_col=0):
            for t in range(NR):
                for j in range(n_src):
                    mm = e.matmul(psF[0:RW, at_col + t:at_col + t + 1], src[:, j, RW * t:RW * t + RW], ones[:, 0:1],
                                  start=(j == 0), stop=(j == n_src - 1))
            return mm

        def on_diagonal(e, sd_sem, rc_sem, dg_sem, count):
            e.wait_ge(sd_sem, count)
            e.reciprocal(rc[0:RW, 0:NR], sd[0:RW, 0:NR]).then_inc(rc_sem, 1)
            e.wait_ge(rc_sem, count)
            e.tensor_tensor(diag[:], ident[0:RW, 0:RW].unsqueeze(1).broadcast_to((RW, NR, RW)),
                            rc[0:RW, 0:NR].unsqueeze(2).broadcast_to((RW, NR, RW)), ALU.mult).then_inc(dg_sem, 1)

        def spread(e, half, psum):
            return e.matmul(psum[:, 0:H2], ones[0:RW, :], diag[:, 3 * half:3 * half + 3, :], start=True, stop=True)

        def norm_stats_pe(e, i):
            e.wait_ge(ssq_done, KT * (i + 1))
            stats(e, ssq[:].unsqueeze(1), 1).then_inc(n_stat, 1)

        def norm_spread_pe(e, i):
            e.wait_ge(n_diag, i + 1)
            spread(e, 0, psA)
            spread(e, 1, psY).then_inc(n_bc, 1)

        def norm_act(e, i):
            e.wait_ge(n_stat, i + 1)
            e.activation(sd[0:RW, 0:NR], psF[0:RW, 0:NR], ACT.Sqrt, scale=1.0 / D,
                         bias=par[0:RW, C_EPS:C_EPS + 1]).then_inc(n_sd, 1)
            e.wait_ge(n_bc, i + 1)
            e.activation(rb[:, 0:H2], psA[:, 0:H2], ACT.Copy)
            e.activation(rb[:, H2:T], psY[:, 0:H2], ACT.Copy).then_inc(n_rb, 1)

        def norm_dve(e, i):
            on_diagonal(e, n_sd, n_rc, n_diag, i + 1)
            if i < 4:
                e.wait_ge(n_stat, i + 1)
                e.memset(ssq[:], 0.0).then_inc(ssq_zero, 1)

        def square(e, idx, slot, tile):
            if later((idx + -1).v):
                e.wait_ge(ssq_done, (idx + -1).v)
            e.activation(sqt[:, slot, :], tile, ACT.Square).then_inc(sq_done, 1)

        def add_squares(e, idx, slot):
            e.wait_ge(sq_done, (idx + 1).v)
            if later(idx.v):
                e.wait_ge(ssq_done, idx.v)
            e.tensor_tensor(ssq[:], ssq[:], sqt[:, slot, :], ALU.add).then_inc(ssq_done, 1)

        def residual_act(e, n, m, slot, i, w):
            taken(e, n)
            square(e, m + KT * i, slot, h[:, at(m.v), :].rearrange("p a t -> p (a t)"))
            if w is not None:
                e.activation(uh[:, at(m.v), :].rearrange("p a t -> p (a t)"),
                             h[:, at(m.v), :].rearrange("p a t -> p (a t)"), ACT.Identity,
                             scale=par[:, at((m + C_NORM + 8 * w).v)]).then_inc(u_hi, 1)

        def residual_dve(e, n, done, m, slot, i, w, base):
            e.wait_ge(*done)
            row = h[:, at(m.v), :].rearrange("p a t -> p (a t)")
            src = base[:, at(m.v), :].rearrange("p a t -> p (a t)")
            free(e.tensor_tensor(halves(row), acc_of(n), halves(src), ALU.add), n)
            add_squares(e, m + KT * i, slot)
            if w is not None:
                e.wait_ge(u_hi, (m + KT * i + 1).v)
                e.scalar_tensor_tensor(out=ul[:, at(m.v), :].rearrange("p a t -> p (a t)"), in0=row,
                                       scalar=par[:, at((m + C_NORM + 8 * w).v)],
                                       in1=uh[:, at(m.v), :].rearrange("p a t -> p (a t)").bitcast(F32),
                                       op0=ALU.mult, op1=ALU.subtract).then_inc(u_lo, 1)

        def down_turns(e, tile):
            with e.Fori(0, 3) as i:
                for q in range(2):
                    tile(e, Idx(3 * q, 6, i), Idx(q, 2, i), q)
            for q in range(2):
                tile(e, Idx(18 + 3 * q), Idx(6 + q), q)

        def pair_turns(e, pair):
            with e.Fori(0, 7) as i:
                for q in range(3):
                    pair(e, Idx(2 + 2 * q, 6, i), Idx(1 + q, 3, i), (1 + q) % 3)

        @block.sync
        def _(sp):
            for q in range(4):
                sp.dma_start(h[:, 2 * q:2 * q + 2, :], x_t[:, 2 * q:2 * q + 2, :]).then_inc(x_sem[q], 16)
                if q == 0:
                    sp.dma_start(par[:], par_d).then_inc(par_in, 16)
                    sp.dma_start(con[:], con_d[:, 0:3 * P]).then_inc(con_in, 16)
            sp.dma_start(cong[:], con_d[0:BUCKETS, K_HOT:NCON]).then_inc(cong_in, 16)
            for u in range(3):
                load_unit(sp, Idx(u))
            turns = (UNITS - 3) // 3
            with sp.Fori(0, turns) as i:
                for s in range(3):
                    load_unit(sp, Idx(3 + s, 3, i))
            for u in range(3 + 3 * turns, UNITS):
                load_unit(sp, Idx(u))
            for q in range(4):
                sp.wait_ge(out_f, 2 * q + 2)
                sp.dma_start(out_d[:, 2 * q:2 * q + 2, :], h[:, 2 * q:2 * q + 2, META:T]).then_inc(stored, 16)
            sp.wait_ge(stored, 64)

        def u_in(k, j):
            return k.times(6, U_IN + j)

        def n_in(k, j):
            return k.times(6, N_IN + j)

        def ssd_steps(e, step, between=None):
            step(e, Idx(0), 0, "in", False, False)
            step(e, Idx(1), 1, "in", True, False)
            with e.Fori(0, 3) as i:
                step(e, Idx(2, 2, i), 0, "in", True, True)
                step(e, Idx(3, 2, i), 1, "in", True, True)
            if between:
                between(e)
            step(e, Idx(8), 0, "out", True, True)
            step(e, Idx(9), 1, "out", False, True)

        def out1(k, j):
            m = 6 * (k.first - 8) + j
            return m if m < KT else None

        S_X, S_E, S_S, S_Q, S_P, S_DT, S_ACS, S_DEC, S_DA, S_EXP = range(10)

        def pe_chunk_in(e, g, gp, c):
            t0, q = CH[c]
            if c == 0:
                e.wait_ge(conv_ready, g.mul(4, 4))
            if later(g.mul(NC, c)):
                e.wait_ge(cbm_done, g.mul(NC, c))
            for j, t in enumerate((2, 3, 1)):
                e.transpose(psA[0:q, P * j:P * j + P], cv[:, gp, t, t0:t0 + q], ident)
            e.matmul(psA[0:q, 3 * P:3 * P + q], cv[:, gp, 1, t0:t0 + q], cv[:, gp, 0, t0:t0 + q],
                     start=True, stop=True).then_inc(chunk_t, 1)

        def pe_chunk_out(e, g, gp, c):
            t0, q = CH[c]
            b = (gp + c) % 2
            e.wait_ge(wt_done, g.mul(NC, c + 1))
            e.wait_ge(xst_done, g.mul(NC, c + 1))
            if later(g.mul(NC, c)):
                e.wait_ge(yadd_done, g.mul(NC, c))
            if c:
                e.wait_ge(cs_done, g.mul(NC - 1, c))
                e.wait_ge(st_done, g.mul(NC - 1, c))
            for r in range(HPG):
                dst = psY[64 * (r % 2):64 * (r % 2) + 64, P * (r // 2):P * (r // 2) + q]
                mm = e.matmul(dst, xdt[0:q, b, 64 * r:64 * r + 64], Lm[0:q, b, r, 0:q], start=True, stop=(c == 0))
                if c:
                    mm = e.matmul(dst, state[:, 64 * r:64 * r + 64], Cs[:, b, r, 0:q], start=False, stop=True)
            if c < NC - 1:
                mm = e.matmul(psS[:, 0:HPG * 64], Btok[0:q, b, :], xst[0:q, b, :], start=True, stop=True)
            mm.then_inc(scan_done, 1)

        def pe_step(e, k, kp, units, ssd, fin):
            g, gp, f = k + -1, 1 - kp, k + -2
            for j in range(6):
                if units == "in":
                    multiply(e, u_in(k, j), n_in(k, j), uh, ul)
                elif out1(k, j) is not None:
                    m = out1(k, j)
                    if m == 0:
                        e.wait_ge(f_lo, 1 + 4)
                    multiply(e, Idx(U_OUT1 + m), Idx(N_OUT1 + m), yh, yl)
                if fin and j == 2:
                    e.wait_ge(f_sq, f.mul(1, 1))
                    stats(e, sqt, 2).then_inc(f_stat, 1)
                if fin and j in (3, 4):
                    e.wait_ge(f_diag, f.mul(1, 1))
                    if j == 4:
                        e.wait_ge(f_rb, f.mul(2, 1))
                    spread(e, j - 3, psF).then_inc(f_bc, 1)
                if ssd and j < NC:
                    pe_chunk_in(e, g, gp, j)
                if ssd and j >= 1:
                    pe_chunk_out(e, g, gp, j - 1)
            if k.rate == 0 and k.first == 0:
                e.wait_ge(dt_a, 7)
                e.wait_ge(dt_v, 21)
                for c, (t0, q) in enumerate(CH):
                    for i, src in enumerate((S_ACS, S_DT, S_DEC)):
                        mm = e.transpose(psF[0:q, (3 * c + i) * HEADS:(3 * c + i + 1) * HEADS],
                                         dt_tmp[:, src, t0:t0 + q], ident[0:HEADS, 0:HEADS])
                mm.then_inc(tok_t, 1)

        def act_step(e, k, kp, units, ssd, fin):
            g, gp, f = k + -1, 1 - kp, k + -2
            for j in range(6):
                if units == "in":
                    u, n = u_in(k, j), n_in(k, j)
                    if 1 <= j <= 4:
                        if later(k.mul(4, j)):
                            e.wait_ge(taps_done, k.mul(4, j))
                        if later(k.mul(4, j - 1)):
                            e.wait_ge(conv_ready, k.mul(4, j - 1))
                        e.activation(th[:], cv[:, kp, j - 1, :], ACT.Tanh).then_inc(tanh_done, 1)
                    e.wait_ge(unit_done, (u + 1).v)
                    if j < 4:
                        if later(k.mul(4, j)):
                            e.wait_ge(taps_done, k.mul(4, j))
                        col = k.mul(20, C_CONV + 5 * j)
                        e.activation(halves(rawc[:, TAPS - 1:]), acc_of(n), ACT.Copy).then_inc(raw_copied, 1)
                        if later((k + -1).mul(NC)):
                            e.wait_ge(yadd_done, (k + -1).mul(NC))
                        if later((k + -1).mul(NC - 1)):
                            e.wait_ge(cs_done, (k + -1).mul(NC - 1))
                        free(e.activation(halves(cv[:, kp, j, :]), acc_of(n), ACT.Identity,
                                          scale=par[:, at(col + 3)], bias=par[:, at(col + 4)]), n)
                    else:
                        prev = n + (-1 if j == 5 else -5)
                        if k.rate or prev.first >= N_IN + 4:
                            taken(e, prev)
                        e.activation(halves(zth[:]), acc_of(n), ACT.Tanh, scale=0.5).then_inc(ztanh_done, 1)
                    look_ahead(e, split_hi, u)
                elif out1(k, j) is not None:
                    look_ahead(e, split_hi, Idx(U_OUT1 + out1(k, j)))
                if ssd and j < NC:
                    q, b = CH[j][1], (gp + j) % 2
                    e.wait_ge(seg_done, g.mul(NC, j + 1))
                    e.activation(Lm[0:q, b, :, 0:q], Lm[0:q, b, :, 0:q], ACT.Exp).then_inc(exp_done, 1)
                if fin and j == 1:
                    e.wait_ge(y2_done, f.mul(1, 1))
                    e.activation(sqt[:], y2[:], ACT.Square).then_inc(f_sq, 1)
                if fin and j == 2:
                    e.wait_ge(f_stat, f.mul(1, 1))
                    e.activation(sd[0:RW, 0:NR], psF[0:RW, 0:NR], ACT.Sqrt, scale=1.0 / (2 * P),
                                 bias=par[0:RW, C_EPS + 1:C_EPS + 2]).then_inc(f_sd, 1)
                if fin and j in (3, 4):
                    e.wait_ge(f_bc, f.mul(2, j - 2))
                    e.activation(rb[:, H2 * (j - 3):H2 * (j - 2)], psF[:, 0:H2], ACT.Copy).then_inc(f_rb, 1)
                if fin and j == 5:
                    e.wait_ge(f_yn, f.mul(2, 2))
                    e.activation(yh[:, at(f.mul(2), 2), :], y2[:], ACT.Copy).then_inc(f_hi, 1)
                if ssd and j < NC - 1:
                    load_decay(e, g, gp, j + 1)
                if ssd and j == NC - 1 and units == "in":
                    load_decay(e, g + 1, kp, 0)
                if k.rate == 0 and k.first == 0 and j == 2:
                    dt_tables_act(e)
            if k.rate == 0 and k.first == 0:
                e.wait_ge(scr_out, 32)
                load_decay(e, Idx(0), 0, 0)

        def load_decay(e, g, gp, c):
            t0, q = CH[c]
            b = (gp + c) % 2
            s = g.times(NC, c)
            if later((s + -1).v):
                e.wait_ge(yadd_done, (s + -1).v)
            for i in range(2):
                src = scr[i, at(g.mul(HPG), HPG), t0:t0 + q]
                e.dma_start(bc[:, b, i, :, 0:q], src.unsqueeze(0).broadcast_to((P, HPG, q))).then_inc(bc_in[b], 16)

        def decay_in(e, g, c, b):
            e.wait_ge(bc_in[b], g.times(NC, c).div(2).mul(32, 32))

        def dve_step(e, k, kp, units, ssd, fin):
            g, gp, f = k + -1, 1 - kp, k + -2
            for j in range(6):
                if fin and j == 0:
                    e.wait_ge(yadd_done, f.mul(NC, NC))
                    e.wait_ge(f_lo, f.mul(1, 1))
                    e.tensor_tensor(y2[:], ybuf[:], zs[:, kp], ALU.mult).then_inc(y2_done, 1)
                if ssd and j < NC:
                    t0, q = CH[j]
                    b = (gp + j) % 2
                    heads = at(g.mul(HPG), HPG)
                    e.wait_ge(chunk_t, g.mul(NC, j + 1))
                    if later(g.mul(NC, j - 1)):
                        e.wait_ge(scan_done, g.mul(NC, j - 1))
                    e.tensor_tensor(xdt[0:q, b, :].rearrange("p (r c) -> p r c", r=HPG),
                                    psA[0:q, 0:2 * P].rearrange("p (r c) -> p r c", r=HPG),
                                    tok[0:q, j, 1, heads].unsqueeze(2).broadcast_to((q, HPG, 64)),
                                    ALU.mult).then_inc(xdt_done, 1)
                    e.tensor_copy(Btok[0:q, b, :], psA[0:q, 2 * P:3 * P])
                    e.tensor_tensor(cbm[0:q, b, 0:q], psA[0:q, 3 * P:3 * P + q], mask[0:q, 0:q],
                                    ALU.mult).then_inc(cbm_done, 1)
                    decay_in(e, g, j, b)
                    for r in range(HPG):
                        ins = e.tensor_scalar(Lm[0:q, b, r, 0:q], bc[0:q, b, 0, r, 0:q],
                                              tok[0:q, j, 0, at(g.mul(HPG, r))], 0.0, ALU.subtract, ALU.min)
                    ins.then_inc(seg_done, 1)
                if units == "in" and 1 <= j <= 4:
                    e.wait_ge(tanh_done, k.mul(4, j))
                    e.scalar_tensor_tensor(out=cv[:, kp, j - 1, :], in0=th[:], scalar=1.0, in1=cv[:, kp, j - 1, :],
                                           op0=ALU.add, op1=ALU.mult).then_inc(conv_ready, 1)
                if units == "in":
                    n = n_in(k, j)
                    if j < 4:
                        taken(e, n)
                        for tap, before, after in ((2, None, tap2_done), (1, tap2_done, tap1_done),
                                                   (0, tap1_done, taps_done)):
                            if before:
                                e.wait_ge(before, k.mul(4, j + 1))
                            e.scalar_tensor_tensor(out=cv[:, kp, j, :], in0=rawc[:, tap:tap + T],
                                                   scalar=par[:, at(k.mul(20, C_CONV + 5 * j + tap))],
                                                   in1=cv[:, kp, j, :], op0=ALU.mult, op1=ALU.add
                                                   ).then_inc(after, 1)
                    else:
                        e.wait_ge(ztanh_done, k.mul(2, j - 3))
                        if later((k + -1).v):
                            e.wait_ge(y2_done, (k + -1).v)
                        free(e.scalar_tensor_tensor(out=halves(zs[:, kp, j - 4, :]), in0=halves(zth[:]), scalar=1.0,
                                                    in1=acc_of(n), op0=ALU.add, op1=ALU.mult), n)
                elif out1(k, j) is not None:
                    m = out1(k, j)
                    e.wait_ge(part_in, 16)
                    e.wait_ge(unit_done, U_OUT1 + m + 1)
                    free(e.tensor_tensor(halves(part[:, m, :]), acc_of(Idx(N_OUT1 + m)), halves(part[:, m, :]),
                                         ALU.add), Idx(N_OUT1 + m))
                if ssd and j >= 1:
                    c = j - 1
                    t0, q = CH[c]
                    b = (gp + c) % 2
                    e.wait_ge(scan_done, g.mul(NC, c + 1))
                    if c == 0:
                        e.tensor_copy(state[:], psS[:, 0:HPG * 64]).then_inc(st_done, 1)
                    elif c < NC - 1:
                        e.wait_ge(st_done, g.mul(NC - 1, c))
                        e.tensor_tensor(stmp[:].rearrange("p (r c) -> p r c", r=HPG),
                                        state[:].rearrange("p (r c) -> p r c", r=HPG),
                                        bc[:, b, 1, :, q - 1:q].broadcast_to((P, HPG, 64)),
                                        ALU.mult).then_inc(stmp_done, 1)
                        e.wait_ge(stmp_done, g.mul(NC - 2, c))
                        e.tensor_tensor(state[:], psS[:, 0:HPG * 64], stmp[:], ALU.add).then_inc(st_done, 1)
                    if c == 0:
                        if later(g.v):
                            e.wait_ge(y2_done, g.v)
                    for i in range(2):
                        ins = e.scalar_tensor_tensor(out=ybuf[:, i, t0:t0 + q], in0=cv[:, gp, 2 + i, t0:t0 + q],
                                                     scalar=par[:, at(g.mul(2, C_DSKIP + i))],
                                                     in1=psY[:, P * i:P * i + q], op0=ALU.mult, op1=ALU.add)
                    ins.then_inc(yadd_done, 1)
                if ssd and j < NC:
                    q, b = CH[j][1], (gp + j) % 2
                    e.wait_ge(exp_done, g.mul(NC, j + 1))
                    e.wait_ge(cbm_done, g.mul(NC, j + 1))
                    e.tensor_tensor(Lm[0:q, b, :, 0:q], Lm[0:q, b, :, 0:q],
                                    cbm[0:q, b, 0:q].unsqueeze(1).broadcast_to((q, HPG, q)),
                                    ALU.mult).then_inc(wt_done, 1)
                if fin and j == 2:
                    on_diagonal(e, f_sd, f_rc, f_diag, f.mul(1, 1))
                if fin and j == 5:
                    e.wait_ge(f_rb, f.mul(2, 2))
                    for i in range(2):
                        e.scalar_tensor_tensor(out=y2[:, i, :], in0=y2[:, i, :],
                                               scalar=par[:, at(f.mul(2, C_SSMN + i))], in1=rb[:],
                                               op0=ALU.mult, op1=ALU.mult).then_inc(f_yn, 1)
                    e.wait_ge(f_hi, f.mul(1, 1))
                    e.tensor_tensor(yl[:, at(f.mul(2), 2), :], y2[:],
                                    yh[:, at(f.mul(2), 2), :].bitcast(F32), ALU.subtract).then_inc(f_lo, 1)
                if k.rate == 0 and k.first == 0 and j == 1:
                    dt_second(e)
            if k.rate == 0 and k.first == 0:
                e.wait_ge(tok_t, 1)
                e.tensor_copy(tok[0:META, 0, :, :], psF[0:META, 0:3 * HEADS].rearrange("p (i h) -> p i h", i=3))
                e.tensor_copy(tok[:, 1:NC, :, :],
                              psF[:, 3 * HEADS:3 * NC * HEADS].rearrange("p (c i h) -> p c i h", i=3, h=HEADS)
                              ).then_inc(tok_ready, 1)
                e.wait_ge(tok_ready, 1)

        def dt_first(e):
            t = lambda i: dt_tmp[:, i, :]
            e.wait_ge(unit_done, 1)
            free(e.tensor_scalar(halves(t(S_X)), acc[0][0:HEADS, :, 0:H2], par[0:HEADS, C_DTB:C_DTB + 1], None,
                                 ALU.add), Idx(0))
            taken(e, Idx(0))
            e.scalar_tensor_tensor(out=t(S_E), in0=t(S_X), scalar=-1.0, in1=t(S_X), op0=ALU.mult,
                                   op1=ALU.min).then_inc(dt_v, 1)
            e.wait_ge(dt_a, 2)
            e.tensor_scalar(t(S_S), t(S_E), 2.0, None, ALU.add).then_inc(dt_v, 1)
            e.wait_ge(dt_v, 2)
            e.reciprocal(t(S_Q), t(S_S)).then_inc(dt_v, 1)
            e.wait_ge(dt_v, 3)
            e.tensor_tensor(t(S_S), t(S_E), t(S_Q), ALU.mult).then_inc(dt_v, 1)
            e.wait_ge(dt_v, 4)
            e.tensor_tensor(t(S_Q), t(S_S), t(S_S), ALU.mult).then_inc(dt_v, 1)
            e.wait_ge(dt_v, 5)
            e.tensor_scalar(t(S_P), t(S_Q), ATANH[0], None, ALU.mult).then_inc(dt_v, 1)

        def dt_second(e):
            t = lambda i: dt_tmp[:, i, :]
            done = 6
            for c in ATANH[1:]:
                e.wait_ge(dt_v, done)
                e.scalar_tensor_tensor(out=t(S_P), in0=t(S_P), scalar=c, in1=t(S_Q), op0=ALU.add,
                                       op1=ALU.mult).then_inc(dt_v, 1)
                done += 1
            e.wait_ge(dt_v, done)
            e.scalar_tensor_tensor(out=t(S_P), in0=t(S_P), scalar=1.0, in1=t(S_S), op0=ALU.add,
                                   op1=ALU.mult).then_inc(dt_v, 1)
            e.tensor_scalar(t(S_X), t(S_X), 0.0, None, ALU.max).then_inc(dt_v, 1)
            e.wait_ge(dt_v, done + 2)
            e.scalar_tensor_tensor(out=t(S_DT), in0=t(S_P), scalar=2.0, in1=t(S_X), op0=ALU.mult,
                                   op1=ALU.add).then_inc(dt_v, 1)
            e.wait_ge(dt_v, done + 3)
            e.wait_ge(dt_a, 1)
            e.tensor_scalar(t(S_DA), t(S_DT), negA[:, 0:1], -1.0, ALU.mult, ALU.mult).then_inc(dt_v, 1)
            e.wait_ge(dt_v, done + 4)
            for t0, q in CH:
                e.tensor_tensor_scan(dt_tmp[:, S_ACS, t0:t0 + q], dt_tmp[:, S_DA, t0:t0 + q],
                                     par[0:HEADS, C_ZERO:C_ZERO + 1].broadcast_to((HEADS, q)), 0.0,
                                     ALU.add, ALU.add).then_inc(dt_v, 1)
            assert done + 4 + NC == 21

        def dt_exp_act(e):
            e.wait_ge(dt_v, 1)
            e.activation(dt_tmp[:, S_E, :], dt_tmp[:, S_E, :], ACT.Exp).then_inc(dt_a, 1)

        def dt_tables_act(e):
            e.wait_ge(dt_v, 21)
            for t0, q in CH:
                e.activation(dt_tmp[:, S_DEC, t0:t0 + q], dt_tmp[:, S_ACS, t0:t0 + q], ACT.Exp, scale=-1.0,
                             bias=dt_tmp[:, S_ACS, t0 + q - 1:t0 + q]).then_inc(dt_a, 1)
            e.activation(dt_tmp[:, S_EXP, :], dt_tmp[:, S_ACS, :], ACT.Exp).then_inc(dt_a, 1)
            e.dma_start(scr[0], dt_tmp[:, S_ACS, :]).then_inc(scr_out, 16)
            e.wait_ge(dt_a, 8)
            e.dma_start(scr[1], dt_tmp[:, S_EXP, :]).then_inc(scr_out, 16)

        def pool_step(e, k, kp, units, ssd, fin):
            g, gp = k + -1, 1 - kp
            if ssd:
                if k.rate == 0 and k.first == 1:
                    e.wait_ge(tok_ready, 1)
                e.tensor_copy(decg[:, gp], tok[:, :, 2, at(g.mul(HPG), HPG)]).then_inc(decg_done, 1)
            for j in range(6):
                if ssd and j < NC:
                    q, b = CH[j][1], (gp + j) % 2
                    e.wait_ge(decg_done, g.mul(1, 1))
                    if later(g.mul(NC, j - 1)):
                        e.wait_ge(scan_done, g.mul(NC, j - 1))
                    e.wait_ge(xdt_done, g.mul(NC, j + 1))
                    e.tensor_tensor(xst[0:q, b, :].rearrange("p (r c) -> p r c", r=HPG),
                                    xdt[0:q, b, :].rearrange("p (r c) -> p r c", r=HPG),
                                    decg[0:q, gp, j, :].unsqueeze(2).broadcast_to((q, HPG, 64)),
                                    ALU.mult).then_inc(xst_done, 1)
                if ssd and 1 <= j < NC:
                    q, b = CH[j][1], (gp + j) % 2
                    decay_in(e, g, j, b)
                    e.wait_ge(conv_ready, g.mul(4, 4))
                    e.tensor_tensor(Cs[:, b, :, 0:q], bc[:, b, 1, :, 0:q],
                                    cv[:, gp, 0, CH[j][0]:CH[j][0] + q].unsqueeze(1).broadcast_to((P, HPG, q)),
                                    ALU.mult).then_inc(cs_done, 1)
                if units == "in":
                    look_ahead(e, split_lo, u_in(k, j))
                elif out1(k, j) is not None:
                    look_ahead(e, split_lo, Idx(U_OUT1 + out1(k, j)))

        def dve_pair(e, u, n, i, slot, ff):
            tot = i + FT * ff
            e.wait_ge(unit_done, (u + 1).v)
            free(e.tensor_tensor(halves(gb[:, slot, :]), acc_of(n), halves(rb[:]), ALU.mult), n)
            e.wait_ge(unit_done, (u + 2).v)
            free(e.tensor_tensor(halves(vb[:, slot, :]), acc_of(n + 1), halves(rb[:]), ALU.mult), n + 1)
            e.wait_ge(silu_done, (tot + 1).v)
            taken(e, n + 1)
            e.tensor_tensor(vb[:, slot, :], vb[:, slot, :], gb[:, slot, :], ALU.mult).then_inc(hid_done, 1)
            e.wait_ge(hid_hi, (tot + 1).v)
            row = hl[:, at(i.v), :].rearrange("p a t -> p (a t)")
            e.tensor_tensor(row, vb[:, slot, :], hh[:, at(i.v), :].rearrange("p a t -> p (a t)").bitcast(F32),
                            ALU.subtract).then_inc(hid_lo, 1)

        def act_pair(e, u, n, i, slot, ff):
            tot = i + FT * ff
            taken(e, n)
            e.activation(gb[:, slot, :], gb[:, slot, :], ACT.Silu).then_inc(silu_done, 1)
            look_ahead(e, split_hi, u)
            look_ahead(e, split_hi, u + 1)
            e.wait_ge(hid_done, (tot + 1).v)
            e.activation(hh[:, at(i.v), :].rearrange("p a t -> p (a t)"), vb[:, slot, :],
                         ACT.Copy).then_inc(hid_hi, 1)

        def pe_ffn(e, u0, n0, u1, n1, ff, i):
            multiply(e, Idx(u0), Idx(n0), uh, ul, moving=(u_lo, KT * i))
            norm_stats_pe(e, i)
            multiply(e, Idx(u0 + 1), Idx(n0 + 1), uh, ul, slices=range(0, 4))
            norm_spread_pe(e, i)
            multiply(e, Idx(u0 + 1), Idx(n0 + 1), uh, ul, slices=range(4, KT))

            def pair(e, du, t, slot):
                multiply(e, du + u0, du + n0, uh, ul)
                multiply(e, du + (u0 + 1), du + (n0 + 1), uh, ul)

            pair_turns(e, pair)
            e.wait_ge(hid_lo, FT * (ff + 1))

            def tile(e, du, m, slot):
                for t, ks in enumerate((KT, KT, FT - 2 * KT)):
                    multiply(e, du + (u1 + t), m + n1, hh, hl, k0=KT * t, ks=ks, first=(t == 0), last=(t == 2))

            down_turns(e, tile)

        def act_ffn(e, u0, n0, u1, n1, ff, i, w):
            norm_act(e, i)
            act_pair(e, Idx(u0), Idx(n0), Idx(0), 0, ff)
            pair_turns(e, lambda e, du, t, slot: act_pair(e, du + u0, du + n0, t, slot, ff))

            def tile(e, du, m, slot):
                for t in range(3):
                    look_ahead(e, split_hi, du + (u1 + t))
                residual_act(e, m + n1, m, slot, i + 1, w)

            down_turns(e, tile)

        def dve_ffn(e, u0, n0, u1, n1, ff, i, w):
            norm_dve(e, i)
            e.wait_ge(n_rb, i + 1)
            e.wait_ge(ssq_zero, i + 1)
            dve_pair(e, Idx(u0), Idx(n0), Idx(0), 0, ff)
            pair_turns(e, lambda e, du, t, slot: dve_pair(e, du + u0, du + n0, t, slot, ff))

            def tile(e, du, m, slot):
                residual_dve(e, m + n1, (unit_done, (du + (u1 + 3)).v), m, slot, i + 1, w, h)

            down_turns(e, tile)

        def pool_ffn(e, u0, u1):
            for t in range(2):
                look_ahead(e, split_lo, Idx(u0 + t))

            def pair(e, du, t, slot):
                look_ahead(e, split_lo, du + u0)
                look_ahead(e, split_lo, du + (u0 + 1))

            def tile(e, du, m, slot):
                for t in range(3):
                    look_ahead(e, split_lo, du + (u1 + t))

            pair_turns(e, pair)
            down_turns(e, tile)

        BLOCKS = [4, 3, 2, 1, 0]
        ORDER = [("s", 0, 0), ("x", 0, 0, 2), ("fq",), ("s", 0, 1), ("vt",), ("x", 0, 2, 4), ("c", 0), ("s", 1, 0),
                 ("s", 1, 1), ("x", 0, 4, 6), ("t", 0), ("x", 0, 6, 8), ("end", 0), ("o", 0), ("fs",), ("c", 1),
                 ("s", 2, 0), ("s", 2, 1), ("x", 1, 0, 2), ("fd",), ("t", 1), ("x", 1, 2, 4), ("fb",), ("o", 1),
                 ("c", 2), ("s", 3, 0), ("s", 3, 1), ("x", 1, 4, 6), ("t", 2), ("fw",), ("x", 1, 6, 8), ("end", 1),
                 ("o", 2), ("c", 3), ("s", 4, 0), ("s", 4, 1), ("x", 2, 0, 2), ("t", 3), ("fl",), ("x", 2, 2, 4),
                 ("o", 3), ("c", 4), ("x", 2, 4, 6), ("t", 4), ("x", 2, 6, 8), ("end", 2), ("o", 4)]
        FB_AFTER = 3

        def att_steps(e, step, first):
            first(e)
            step(e, Idx(1), 1, True, True, False)
            with e.Fori(0, 3) as i:
                step(e, Idx(2, 2, i), 0, True, True, True)
                step(e, Idx(3, 2, i), 1, True, True, True)
            step(e, Idx(8), 0, False, True, True)
            step(e, Idx(9), 1, False, False, True)

        def u_att(k, j):
            return k.times(3, U_KVQ + j)

        def n_att(k, j):
            return k.times(3, N_KVQ + j)

        def early_slices(k, ev):
            _, j, a, b = ev
            if k.first == 8:
                return range(3 * (8 * j + a) // 2, 3 * (8 * j + b) // 2)
            return range(36 + 3 * a // 2, 36 + 3 * b // 2) if j == 2 else range(0)

        def early_done(k, ev):
            return [s // EARLY for s in early_slices(k, ev) if s % EARLY == EARLY - 1]

        def pe_att(e, k, kp, units, att, fin):
            g, gp, f = k + -1, 1 - kp, k + -2
            for ev in ORDER:
                what = ev[0]
                if what == "x" and units:
                    j = ev[1]
                    multiply(e, u_att(k, j), n_att(k, j), kh if j else uh, kl if j else ul,
                             slices=range(ev[2], ev[3]))
                elif what == "x":
                    for s in early_slices(k, ev):
                        m = s // EARLY
                        if s == 0:
                            e.wait_ge(h_lo, EARLY)
                        multiply(e, Idx(U_O1 + m), Idx(N_O1 + m), oTh, oTl, ks=EARLY,
                                 slices=range(s % EARLY, s % EARLY + 1))
                elif what == "vt" and att:
                    taken(e, n_att(g, 2))
                    if later(g.mul(NC)):
                        e.wait_ge(p_tc, g.mul(NC))
                    if later(g.mul(NC)):
                        e.wait_ge(o_out, g.mul(NC))
                    for c in range(1, NC):
                        t0, q = CH[c]
                        e.transpose(psS[0:q, P * (c - 1):P * c], vT[:, t0:t0 + q], ident)
                    e.transpose(psF[0:META, P:2 * P], vT[:, 0:META], ident).then_inc(v_t, 1)
                elif what == "s" and att:
                    _, i, c = ev
                    t0, q = CH[BLOCKS[i]]
                    rows = slice(64 * c, 64 * c + 64)
                    if i == 0:
                        if c == 0:
                            taken(e, n_att(g, 0))
                            taken(e, n_att(g, 1))
                        if later(g.mul(2 * NC, c)):
                            e.wait_ge(s_max, g.mul(2 * NC, c))
                        for half in range(2):
                            mm = e.matmul(psAY[:, half, 0:H2], qT[rows, gp, t0:t0 + P],
                                          kT[rows, gp, H2 * half:H2 * half + H2], start=True, stop=True)
                    else:
                        if i == 1:
                            e.wait_ge(s_max, g.mul(2 * NC, 2))
                        else:
                            e.wait_ge(s_max, g.mul(2 * NC, 2 * i + c - 1))
                        if i == FB_AFTER and c == 0 and fin:
                            e.wait_ge(h_rb, f.mul(1, 1))
                        mm = e.matmul(psAY[:, c, 0:t0 + q], qT[rows, gp, t0:t0 + P], kT[rows, gp, 0:t0 + q],
                                      start=True, stop=True)
                    mm.then_inc(s_mm, 1)
                elif what == "t" and att:
                    i, b = ev[1], BLOCKS[ev[1]]
                    s = (gp + i) % 2
                    e.wait_ge(p_comb, g.mul(NC, i + 1))
                    if later(g.mul(NC, i)):
                        e.wait_ge(p_tc, g.mul(NC, i))
                    if later(g.mul(NC, i)):
                        e.wait_ge(o_out, g.mul(NC, i))
                    if i == 0:
                        e.wait_ge(v_tok, g.mul(1, 1))
                    if i == 1 and fin:
                        e.wait_ge(h_sd, f.mul(1, 1))
                    for c in range(1, b + 1):
                        e.transpose(psS[:, P * (c - 1):P * c], pr[:, s, 0, CH[c][0]:CH[c][0] + P], ident)
                    e.transpose(psF[0:META, P:2 * P], pr[:, s, 0, 0:META], ident).then_inc(p_t, 1)
                elif what == "o" and att:
                    i, b = ev[1], BLOCKS[ev[1]]
                    q, s = CH[b][1], (gp + i) % 2
                    e.wait_ge(p_tc, g.mul(NC, i + 1))
                    for c in range(b + 1):
                        n = CH[c][1]
                        mm = e.matmul(psF[:, 0:q], vtok[0:n, c, :], aT[0:n, s, c, 0:q], start=(c == 0), stop=(c == b))
                    mm.then_inc(o_mm, 1)
                elif what == "fs" and fin:
                    e.wait_ge(h_sq, f.mul(1, 1))
                    e.wait_ge(o_out, g.mul(NC, 1) if att else NC * AH)
                    stats(e, sqt[:, 0:1, :], 1, 2 * P).then_inc(h_stat, 1)
                elif what == "fb" and fin:
                    e.wait_ge(h_diag, f.mul(1, 1))
                    e.wait_ge(s_max, g.mul(2 * NC, 2 * FB_AFTER if att else 0))
                    spread(e, 0, psA)
                    spread(e, 1, psY).then_inc(h_bc, 1)

        def pe_att_first(e):
            multiply(e, Idx(U_KVQ), Idx(N_KVQ), uh, ul, moving=(u_lo, 2 * KT))
            norm_stats_pe(e, 2)
            multiply(e, Idx(U_KVQ + 1), Idx(N_KVQ + 1), kh, kl, slices=range(0, 4), moving=(k_lo, 0))
            norm_spread_pe(e, 2)
            multiply(e, Idx(U_KVQ + 1), Idx(N_KVQ + 1), kh, kl, slices=range(4, KT), moving=(k_lo, 0))
            multiply(e, Idx(U_KVQ + 2), Idx(N_KVQ + 2), kh, kl)

        def pe_o2(e):
            e.wait_ge(h_lo, AH)
            for m in range(KT):
                n, u = Idx(N_O2 + m), Idx(U_O2 + m // 4)
                s, a = u.first % 3, acc[n.first % 2]
                e.wait_ge(lo_ready, u.first + 1)
                if later(n.div(2).v):
                    e.wait_ge(acc_free[n.first % 2], n.div(2).v)
                for c in range(AH - EARLY):
                    k = 2 * (m % 4) + c
                    for i, (wt, mv) in enumerate(((wh, oTh), (wh, oTl), (wl, oTh))):
                        for half in range(2):
                            mm = e.matmul(a[:, half, 0:H2], wt[s][:, k, :],
                                          mv[:, EARLY + c, H2 * half:H2 * half + H2],
                                          start=(c == 0 and i == 0), stop=(c == 1 and i == 2))
                mm.then_inc(unit_done if m % 4 == 3 else o2_mm, 1)

        def o2_done(m):
            return (unit_done, U_O2 + m // 4 + 1) if m % 4 == 3 else (o2_mm, m - m // 4 + 1)

        def load_bias(e, g, gp):
            if later((g + -1).mul(2 * NC)):
                e.wait_ge(s_max, (g + -1).mul(2 * NC))
            e.dma_start(bias[:, gp, :], skewed(g)).then_inc(bias_in[gp], 16)

        def skewed(g):
            row = scr_b[at(g.v), :]
            return bass.AP(row.tensor, row.offset + P - 1, [[ND - 1, P], [1, T]])

        def act_att(e, k, kp, units, att, fin):
            g, gp, f, fp = k + -1, 1 - kp, k + -2, kp
            for ev in ORDER:
                what = ev[0]
                if what == "fq" and fin:
                    e.wait_ge(o_out, f.mul(NC, NC))
                    e.activation(sqt[:, 0, :], oraw[:, fp, :], ACT.Square).then_inc(h_sq, 1)
                elif what == "end" and units:
                    look_ahead(e, split_hi, u_att(k, ev[1]))
                    if ev[1] == 0:
                        load_bias(e, k, kp)
                elif what == "x" and not units:
                    for m in early_done(k, ev):
                        look_ahead(e, split_hi, Idx(U_O1 + m))
                elif what == "s" and att:
                    _, i, c = ev
                    s, n = (gp + i) % 2, sum(CH[BLOCKS[i]])
                    e.wait_ge(s_max, g.mul(2 * NC, 2 * i + c + 1))
                    e.activation(pr[:, s, c, 0:n], pr[:, s, c, 0:n], ACT.Exp, scale=-1.0,
                                 bias=sm[:, s, c:c + 1], accum_out=sm[:, s, 2 + c:3 + c]).then_inc(p_exp, 1)
                elif what == "t" and att:
                    i, b = ev[1], BLOCKS[ev[1]]
                    q, s = CH[b][1], (gp + i) % 2
                    e.wait_ge(p_t, g.mul(NC, i + 1))
                    if later(g.mul(NC, i - 1)):
                        e.wait_ge(o_mm, g.mul(NC, i - 1))
                    if b:
                        e.activation(aT[:, s, 1:b + 1, :], psS[:, 0:P * b].rearrange("p (c t) -> p c t", c=b), ACT.Copy)
                    e.activation(aT[0:META, s, 0, 0:q], psF[0:META, P:P + q], ACT.Copy).then_inc(p_tc, 1)
                elif what == "fs" and fin:
                    e.wait_ge(h_stat, f.mul(1, 1))
                    e.activation(sd[0:RW, 0:NR], psF[0:RW, 2 * P:2 * P + NR], ACT.Sqrt, scale=1.0 / P,
                                 bias=par[0:RW, C_EPS:C_EPS + 1]).then_inc(h_sd, 1)
                elif what == "fb" and fin:
                    e.wait_ge(h_bc, f.mul(1, 1))
                    e.activation(halves(rb2[:]), psAY[:, :, 0:H2], ACT.Copy).then_inc(h_rb, 1)
                elif what == "fw" and fin:
                    e.wait_ge(h_on, f.mul(1, 1))
                    e.activation(oTh[:, at(f.v), :].rearrange("p a t -> p (a t)"), on[:], ACT.Copy).then_inc(h_hi, 1)

        def act_att_first(e):
            e.wait_ge(unit_done, U_KVQ)
            for k in range(KT):
                e.activation(kh[:, k, :], h[:, k, :], ACT.Identity,
                             scale=par[:, C_NORM + 16 + k:C_NORM + 17 + k]).then_inc(k_hi, 1)
            norm_act(e, 2)
            e.wait_ge(gvec_out, 16)
            load_bias(e, Idx(0), 0)
            for j in range(3):
                look_ahead(e, split_hi, Idx(U_KVQ + j))

        def dve_att(e, k, kp, units, att, fin):
            g, gp, f, fp = k + -1, 1 - kp, k + -2, kp
            for ev in ORDER:
                what = ev[0]
                if what == "end" and units:
                    take_qkv(e, k, kp, ev[1])
                elif what == "x" and not units:
                    for m in early_done(k, ev):
                        n = Idx(N_O1 + m)
                        e.wait_ge(unit_done, U_O1 + m + 1)
                        free(e.tensor_tensor(halves(h[:, m, :]), acc_of(n), halves(h[:, m, :]), ALU.add), n)
                elif what == "vt" and att:
                    e.wait_ge(v_t, g.mul(1, 1))
                    e.tensor_copy(vtok[0:META, 0, :], psF[0:META, P:2 * P])
                    e.tensor_copy(vtok[:, 1:NC, :], psS[:].rearrange("p (c t) -> p c t", c=NC - 1)).then_inc(v_tok, 1)
                elif what == "s" and att:
                    _, i, c = ev
                    t0 = CH[BLOCKS[i]][0]
                    s, n = (gp + i) % 2, sum(CH[BLOCKS[i]])
                    if i == 0 and c == 0:
                        e.wait_ge(bias_in[gp], g.div(2).mul(16, 16))
                    if later(g.mul(NC, i - 1)):
                        e.wait_ge(p_t, g.mul(NC, i - 1))
                    e.wait_ge(s_mm, g.mul(2 * NC, 2 * i + c + 1))
                    e.memset(sm[:, s, 7 + c:8 + c], 0.0)
                    src = bias[:, gp, T - P - t0:T - P - t0 + n]
                    if i:
                        io = pr[:, s, c, 0:n], psAY[:, c, 0:n], src
                    else:
                        io = halves(pr[:, s, c, :]), psAY[:, :, 0:H2], halves(src)
                    e.tensor_tensor_reduce(*io, 1.0, 3e38, ALU.add, ALU.min,
                                           sm[:, s, c:c + 1]).then_inc(s_max, 1)
                elif what == "c" and att:
                    i = ev[1]
                    s, n, done = (gp + i) % 2, sum(CH[BLOCKS[i]]), g.mul(NC, i + 1)
                    e.wait_ge(p_exp, g.mul(2 * NC, 2 * i + 2))
                    e.reciprocal(sm[:, s, 4:6], sm[:, s, 2:4]).then_inc(p_rec, 1)
                    e.wait_ge(p_rec, done)
                    e.tensor_scalar(sm[:, s, 6:7], sm[:, s, 5:6], lam[:, 5:6], None, ALU.mult).then_inc(p_lam, 1)
                    e.tensor_scalar(pr[:, s, 0, 0:n], pr[:, s, 0, 0:n], sm[:, s, 4:5], None,
                                    ALU.mult).then_inc(p_half, 1)
                    e.wait_ge(p_lam, done)
                    e.wait_ge(p_half, done)
                    e.scalar_tensor_tensor(out=pr[:, s, 0, 0:n], in0=pr[:, s, 1, 0:n], scalar=sm[:, s, 6:7],
                                           in1=pr[:, s, 0, 0:n], op0=ALU.mult, op1=ALU.add).then_inc(p_comb, 1)
                elif what == "o" and att:
                    t0, q = CH[BLOCKS[ev[1]]]
                    e.wait_ge(o_mm, g.mul(NC, ev[1] + 1))
                    e.tensor_copy(oraw[:, gp, t0:t0 + q], psF[:, 0:q]).then_inc(o_out, 1)
                elif what == "fd" and fin:
                    on_diagonal(e, h_sd, h_rc, h_diag, f.mul(1, 1))
                elif what == "fw" and fin:
                    e.wait_ge(h_rb, f.mul(1, 1))
                    e.scalar_tensor_tensor(out=on[:], in0=oraw[:, fp, :], scalar=lam[:, 6:7], in1=rb2[:],
                                           op0=ALU.mult, op1=ALU.mult).then_inc(h_on, 1)
                elif what == "fl" and fin:
                    e.wait_ge(h_hi, f.mul(1, 1))
                    e.tensor_tensor(oTl[:, at(f.v), :].rearrange("p a t -> p (a t)"), on[:],
                                    oTh[:, at(f.v), :].rearrange("p a t -> p (a t)").bitcast(F32),
                                    ALU.subtract).then_inc(h_lo, 1)

        def take_qkv(e, k, kp, j):
            n = n_att(k, j)
            e.wait_ge(unit_done, (u_att(k, j) + 1).v)
            if j == 0:
                free(e.scalar_tensor_tensor(out=halves(qT[:, kp, :]), in0=acc_of(n), scalar=-(64 ** -0.5),
                                            in1=halves(rb[:]), op0=ALU.mult, op1=ALU.mult), n)
            else:
                dst = kT[:, kp, :] if j == 1 else vT[:]
                free(e.tensor_tensor(halves(dst), acc_of(n), halves(rb[:]), ALU.mult), n)

        def dve_att_first(e):
            for k in range(KT):
                e.wait_ge(k_hi, k + 1)
                e.scalar_tensor_tensor(out=kl[:, k, :], in0=h[:, k, :], scalar=par[:, C_NORM + 16 + k:C_NORM + 17 + k],
                                       in1=kh[:, k, :].bitcast(F32), op0=ALU.mult, op1=ALU.subtract).then_inc(k_lo, 1)
            norm_dve(e, 2)
            e.wait_ge(n_rb, 3)
            e.wait_ge(ssq_zero, 4)
            for j in range(3):
                take_qkv(e, Idx(0), 0, j)

        def pool_att(e, k, kp, units, att, fin):
            for ev in ORDER:
                if ev[0] == "end" and units:
                    look_ahead(e, split_lo, u_att(k, ev[1]))
                elif ev[0] == "x" and not units:
                    for m in early_done(k, ev):
                        look_ahead(e, split_lo, Idx(U_O1 + m))

        def pool_att_first(e):
            for j in range(3):
                look_ahead(e, split_lo, Idx(U_KVQ + j))

        @block.tensor
        def _(pe):
            pe.wait_ge(con_in, 16)
            pe.wait_ge(setup, 1)
            pe.matmul(psS[:, 0:2], ones[0:64, :], lam[0:64, 0:2], start=True, stop=True).then_inc(lam_mm, 1)
            pe.wait_ge(cong_in, 16)
            pe.wait_ge(par_in, 16)
            pe.matmul(psA[0:AH, 0:512], par[0:BUCKETS, C_REL:C_REL + AH], cong[:, 0:512], start=True, stop=True)
            pe.matmul(psY[0:AH, 0:ND - 512], par[0:BUCKETS, C_REL:C_REL + AH], cong[:, 512:ND],
                      start=True, stop=True).then_inc(hot_mm, 1)
            norm_stats_pe(pe, 0)
            pe.wait_ge(setup, 7)
            norm_spread_pe(pe, 0)
            multiply(pe, Idx(0), Idx(0), uh, ul, moving=(u_lo, 0))
            ssd_steps(pe, pe_step)
            pe.wait_ge(f_lo, 1 + G)
            for m in range(KT):
                multiply(pe, Idx(U_OUT2 + m), Idx(N_OUT2 + m), yh[:, KT:, :], yl[:, KT:, :])
            pe_ffn(pe, U_GU0, N_GU0, U_DN0, N_DN0, 0, 1)
            att_steps(pe, pe_att, pe_att_first)
            pe_o2(pe)
            pe_ffn(pe, U_GU1, N_GU1, U_DN1, N_DN1, 1, 3)
            norm_stats_pe(pe, 4)
            norm_spread_pe(pe, 4)

        @block.scalar
        def _(act):
            act.wait_ge(par_in, 16)
            act.activation(negA[:, 0:1], par[0:HEADS, C_ALOG:C_ALOG + 1], ACT.Exp).then_inc(dt_a, 1)
            act.wait_ge(lam_mm, 1)
            act.activation(lam[:, 2:4], psS[:, 0:2], ACT.Exp).then_inc(lam_exp, 1)
            for k in range(KT):
                act.wait_ge(x_sem[k // 2], 16)
                square(act, Idx(k), k % 2, h[:, k, :])
            act.wait_ge(setup, 7)
            act.dma_start(scr_b.rearrange("h (p m) -> h p m", m=ND),
                          gvec[:].unsqueeze(1).broadcast_to((AH, P, ND))).then_inc(gvec_out, 16)
            norm_act(act, 0)
            for u in range(3):
                split_hi(act, Idx(u))
            for k in range(KT):
                act.wait_ge(u_f, k + 1)
                act.activation(uh[:, k, :], h[:, k, :], ACT.Copy).then_inc(u_hi, 1)
            dt_exp_act(act)
            look_ahead(act, split_hi, Idx(0))

            def step(e, k, kp, units, ssd, fin):
                act_step(e, k, kp, units, ssd, fin)

            def reload(e):
                e.wait_ge(unit_done, U_OUT1)
                e.dma_start(part[:], x_t).then_inc(part_in, 16)

            ssd_steps(act, step, reload)
            for m in range(KT):
                look_ahead(act, split_hi, Idx(U_OUT2 + m))
                residual_act(act, Idx(N_OUT2 + m), Idx(m), m % 2, 1, 1)
            act_ffn(act, U_GU0, N_GU0, U_DN0, N_DN0, 0, 1, 3)
            att_steps(act, act_att, act_att_first)
            for m in range(KT):
                if m % 4 == 3:
                    look_ahead(act, split_hi, Idx(U_O2 + m // 4))
                residual_act(act, Idx(N_O2 + m), Idx(m), m % 2, 3, 4)
            act_ffn(act, U_GU1, N_GU1, U_DN1, N_DN1, 1, 3, None)
            norm_act(act, 4)

        @block.vector
        def _(dve):
            dve.wait_ge(par_in, 16)
            dve.tensor_tensor(lam[0:64, 0:2], par[0:64, C_LAM:C_LAM + 2], par[0:64, C_LAM + 2:C_LAM + 4],
                              ALU.mult).then_inc(setup, 1)
            dve.tensor_scalar(par[:, C_CONV:C_SUBLN], par[:, C_CONV:C_SUBLN], 0.5, None, ALU.mult).then_inc(setup, 1)
            dve.tensor_scalar(lam[:, 6:7], par[:, C_SUBLN:C_SUBLN + 1], 1.0 - LAMBDA_INIT, None,
                              ALU.mult).then_inc(setup, 1)
            dve.memset(ssq[:], 0.0).then_inc(ssq_zero, 1)
            dve.memset(rawc[:, 0:TAPS - 1], 0.0)
            dve.memset(tok[:], 0.0).then_inc(f_lo, 1)
            dve.wait_ge(lam_exp, 1)
            dve.tensor_tensor(lam[:, 4:5], lam[:, 3:4], lam[:, 2:3], ALU.subtract).then_inc(setup, 1)
            dve.wait_ge(setup, 4)
            dve.tensor_scalar(lam[:, 5:6], lam[:, 4:5], -LAMBDA_INIT, None, ALU.add).then_inc(setup, 1)
            dve.wait_ge(hot_mm, 1)
            dve.scalar_tensor_tensor(out=gvec[:, 0:512], in0=psA[0:AH, 0:512], scalar=-1.0,
                                     in1=cong[0:AH, ND:ND + 512], op0=ALU.mult, op1=ALU.add).then_inc(setup, 1)
            dve.scalar_tensor_tensor(out=gvec[:, 512:ND], in0=psY[0:AH, 0:ND - 512], scalar=-1.0,
                                     in1=cong[0:AH, ND + 512:2 * ND], op0=ALU.mult, op1=ALU.add).then_inc(setup, 1)
            dve.wait_ge(ssq_zero, 1)
            for k in range(KT):
                add_squares(dve, Idx(k), k % 2)
            norm_dve(dve, 0)
            dve.wait_ge(n_rb, 1)

            def lo_of(k):
                dve.wait_ge(u_hi, k + 1)
                dve.tensor_tensor(ul[:, k, :], h[:, k, :], uh[:, k, :].bitcast(F32), ALU.subtract).then_inc(u_lo, 1)

            for k in range(KT):
                dve.scalar_tensor_tensor(out=h[:, k, :], in0=h[:, k, :], scalar=par[:, C_NORM + k:C_NORM + k + 1],
                                         in1=rb[:], op0=ALU.mult, op1=ALU.mult).then_inc(u_f, 1)
                if k:
                    lo_of(k - 1)
            lo_of(KT - 1)
            dt_first(dve)
            ssd_steps(dve, dve_step)
            dve.wait_ge(ssq_zero, 2)
            for m in range(KT):
                residual_dve(dve, Idx(N_OUT2 + m), (unit_done, U_OUT2 + m + 1), Idx(m), m % 2, 1, 1, part)
            dve_ffn(dve, U_GU0, N_GU0, U_DN0, N_DN0, 0, 1, 3)
            att_steps(dve, dve_att, dve_att_first)
            for m in range(KT):
                residual_dve(dve, Idx(N_O2 + m), o2_done(m), Idx(m), m % 2, 3, 4, h)
            dve_ffn(dve, U_GU1, N_GU1, U_DN1, N_DN1, 1, 3, None)
            norm_dve(dve, 4)
            dve.wait_ge(n_rb, 5)
            for k in range(KT):
                dve.scalar_tensor_tensor(out=h[:, k, :], in0=h[:, k, :],
                                         scalar=par[:, C_NORM + 40 + k:C_NORM + 41 + k], in1=rb[:],
                                         op0=ALU.mult, op1=ALU.mult).then_inc(out_f, 1)

        @block.gpsimd
        def _(pool):
            for u in range(3):
                split_lo(pool, Idx(u))
            look_ahead(pool, split_lo, Idx(0))
            ssd_steps(pool, pool_step)
            for m in range(KT):
                look_ahead(pool, split_lo, Idx(U_OUT2 + m))
            pool_ffn(pool, U_GU0, U_DN0)
            att_steps(pool, pool_att, pool_att_first)
            for u in range(2):
                look_ahead(pool, split_lo, Idx(U_O2 + u))
            pool_ffn(pool, U_GU1, U_DN1)


def buckets():
    n = np.maximum(np.array(DIST), 0)
    exact = BUCKETS // 2
    nf = np.maximum(n, 1).astype(np.float32)
    large = exact + (np.log(nf / np.float32(exact)) / np.float32(math.log(MAX_DIST / exact))
                     * np.float32(BUCKETS - exact)).astype(np.int32)
    return np.where(n < exact, n, np.minimum(large, BUCKETS - 1))


def constants():
    con = np.zeros((P, NCON), np.float32)
    con[:, K_ONES:K_ONES + P] = 1.0
    con[:, K_ID:K_ID + P] = np.eye(P)
    con[:, K_MASK:K_MASK + P] = np.triu(np.ones((P, P)))
    con[buckets(), K_HOT + np.arange(ND)] = 1.0
    con[:, K_POS:K_POS + ND] = np.where(np.array(DIST) < 0, 1e30, 0.0)
    return con


def lay_out(a):
    w = np.zeros((UNITS, P, KT, P), np.float32)

    def put(u, block):
        ks = block.shape[0] // P
        w[u, :, :ks, :block.shape[1]] = block.reshape(ks, P, block.shape[1]).transpose(1, 0, 2)

    w_in, w_out = a["ssm_in_w"][0], a["ssm_out_w"][0]
    col = lambda m, t: m[:, P * t:P * t + P]
    put(0, w_in[:, 6144:])
    for g in range(G):
        for j, t in enumerate((40 + g, 32 + g, 16 + 2 * g, 17 + 2 * g, 2 * g, 2 * g + 1)):
            put(U_IN + 6 * g + j, col(w_in, t))
    for m in range(KT):
        put(U_OUT1 + m, col(w_out[:D], m))
        put(U_OUT2 + m, col(w_out[D:], m))
    for u_gu, u_dn, layer in ((U_GU0, U_DN0, 0), (U_GU1, U_DN1, 1)):
        gu, down = a["ffn_w_gu"][layer], a["ffn_w_down"][layer]
        for i in range(FT):
            put(u_gu + 2 * i, col(gu, i))
            put(u_gu + 2 * i + 1, col(gu, FT + i))
        for m in range(KT):
            for t in range(3):
                put(u_dn + 3 * m + t, col(down[D * t:D * (t + 1)], m))
    for hd in range(AH):
        put(U_KVQ + 3 * hd, col(a["w_q"][0], hd))
        put(U_KVQ + 3 * hd + 1, col(a["w_kv"], hd))
        put(U_KVQ + 3 * hd + 2, col(a["w_kv"], AH + hd))
    w_o = a["w_o"][0]
    for m in range(KT):
        put(U_O1 + m, col(w_o[:EARLY * P], m))
        for i in range(AH - EARLY):
            w[U_O2 + m // 4, :, 2 * (m % 4) + i, :] = col(w_o[(EARLY + i) * P:(EARLY + i + 1) * P], m)

    tiles = lambda v: v.reshape(-1, P).T
    par = np.zeros((P, NPAR), np.float32)
    for i, v in enumerate((a["norm_w"][0, 0], a["norm_w"][0, 1], a["kv_norm_w"], a["norm_w"][1, 0],
                           a["norm_w"][1, 1], a["final_norm_w"])):
        par[:, C_NORM + 8 * i:C_NORM + 8 * i + 8] = tiles(v)
    par[:, C_SSMN:C_SSMN + 16] = tiles(a["ssm_norm_w"][0])
    par[:, C_DSKIP:C_DSKIP + 16] = tiles(np.repeat(a["ssm_d"][0], 64))
    cw, cb = a["ssm_conv_w"][0], a["ssm_conv_b"][0]
    for g in range(G):
        for j, t in enumerate((24 + g, 16 + g, 2 * g, 2 * g + 1)):
            c = C_CONV + (4 * g + j) * 5
            par[:, c:c + 4] = cw[:, P * t:P * t + P].T
            par[:, c + 4] = cb[P * t:P * t + P]
    par[:, C_SUBLN] = a["subln_w"][0]
    par[:HEADS, C_DTB] = a["ssm_dt_bias"][0]
    par[:HEADS, C_ALOG] = a["ssm_a_log"][0]
    for i, name in enumerate(("lam_q1", "lam_q2", "lam_k1", "lam_k2")):
        par[:64, C_LAM + i] = a[name][0]
    par[:BUCKETS, C_REL:C_REL + AH] = a["rel_bias"]
    par[:, C_EPS] = EPS
    par[:, C_EPS + 1] = 4 * EPS

    x = np.concatenate([a["meta_tokens"], a["x"][0]], axis=0)
    x_t = np.ascontiguousarray(x.T.reshape(KT, P, T).transpose(1, 0, 2))
    return {"w_all": w.reshape(UNITS, P, KT * P), "x_t": x_t, "par": par, "con": constants()}


def kernel(**inputs):
    import concourse.bacc as bacc
    from concourse.bass_utils import run_bass_kernel_spmd

    nc = bacc.Bacc("TRN2", target_bir_lowering=False, num_devices=1, dynamic_dma_scratch_size=1024)
    arrays = lay_out({k: np.asarray(v) for k, v in inputs.items()})
    args = [nc.dram_tensor(f"{n}_dram", arrays[n].shape, F32, kind="ExternalInput").ap()
            for n in ("w_all", "x_t", "par", "con")]
    out = nc.dram_tensor("out_dram", (P, KT, SEQ), F32, kind="ExternalOutput").ap()
    build(nc, *args, out)
    r = run_bass_kernel_spmd(nc, [{f"{n}_dram": v for n, v in arrays.items()}], core_ids=[0])
    got = np.asarray(r.results[0]["out_dram"])
    return np.ascontiguousarray(got.transpose(2, 1, 0).reshape(1, SEQ, D))
```

```python
import math
from contextlib import ExitStack

import numpy as np

import concourse.bass as bass
from concourse import mybir

F32 = mybir.dt.float32
F32R = mybir.dt.float32r
ALU = mybir.AluOpType
ACT = mybir.ActivationFunctionType

P = 128
D = 1024
KT = D // P
META, SEQ = 16, 512
T = META + SEQ
H2 = T // 2
G, HPG = 8, 4
HEADS = G * HPG
TAPS = 4
FT = 22
AH = 8
SPLIT_BLOCKS = 3
POOLED = 3
EARLY = 6
EPS = 1e-6
LAMBDA_INIT = 0.8 - 0.6 * math.exp(-0.3 * 1)
BUCKETS, MAX_DIST = 32, 128
CH = [(0, META)] + [(META + P * i, P) for i in range(SEQ // P)]
NC = len(CH)
NR, RW = 6, T // 6
DIST = [T - 1 - m for m in range(T - 1 + P)]
ND = len(DIST)

U_IN, N_IN = 1, 1
U_OUT1, N_OUT1 = U_IN + 6 * G, N_IN + 6 * G
U_OUT2, N_OUT2 = U_OUT1 + KT, N_OUT1 + KT
U_GU0, N_GU0 = U_OUT2 + KT, N_OUT2 + KT
U_DN0, N_DN0 = U_GU0 + 2 * FT, N_GU0 + 2 * FT
U_KVQ, N_KVQ = U_DN0 + 3 * KT, N_DN0 + KT
U_O1, N_O1 = U_KVQ + 3 * AH, N_KVQ + 3 * AH
U_O2, N_O2 = U_O1 + KT, N_O1 + KT
U_GU1, N_GU1 = U_O2 + 2, N_O2 + KT
U_DN1, N_DN1 = U_GU1 + 2 * FT, N_GU1 + 2 * FT
UNITS = U_DN1 + 3 * KT

C_NORM = 0
C_SSMN = C_NORM + 48
C_DSKIP = C_SSMN + 16
C_CONV = C_DSKIP + 16
C_SUBLN = C_CONV + 4 * G * 5
C_DTB = C_SUBLN + 1
C_ALOG = C_DTB + 1
C_LAM = C_ALOG + 1
C_REL = C_LAM + 4
C_EPS = C_REL + AH
C_ZERO = C_EPS + 2
NPAR = C_ZERO + 1
K_ONES, K_ID, K_MASK, K_HOT = 0, P, 2 * P, 3 * P
K_POS = K_HOT + ND
NCON = K_POS + ND

ATANH = [1 / 15, 1 / 13, 1 / 11, 1 / 9, 1 / 7, 1 / 5, 1 / 3]
DT_STEPS = 21


def later(count):
    return not isinstance(count, int) or count > 0


def at(i, n=1):
    return slice(i, i + n) if isinstance(i, int) else bass.ds(i, n)


def build(nc, w_all, x_t, par_d, con_d, out_d):
    ctx = ExitStack()
    with ctx:
        base = (nc.sbuf_base + 63) // 64 * 64
        top = nc.sbuf_usable_end

        def place(name, shape, dt, off):
            size = 4 * int(np.prod(shape[1:]))
            assert base + off + size <= top, (name, base + off + size - top)
            return nc.alloc_sbuf_tensor_at(name, shape, dt, offset=base + off), off + (size + 31) // 32 * 32

        def sem(name):
            return ctx.enter_context(nc.semaphore(name))

        o = 0
        uh, o = place("uh", [P, KT, T], F32R, o)
        ul, o = place("ul", [P, KT, T], F32R, o)
        raw, wh, wl = [], [], []
        for s in range(3):
            t, o = place(f"raw{s}", [P, KT, P], F32, o)
            raw.append(t)
            t, o = place(f"wh{s}", [P, KT, P], F32R, o)
            wh.append(t)
            t, o = place(f"wl{s}", [P, KT, P], F32R, o)
            wl.append(t)
        ssq, o = place("ssq", [P, T], F32, o)
        sqt, o = place("sqt", [P, 2, T], F32, o)
        rb, o = place("rb", [P, T], F32, o)
        diagh, o = place("diagh", [RW, NR, RW], F32R, o)
        diagl, o = place("diagl", [RW, NR, RW], F32R, o)
        ones_r, o = place("ones_r", [P, P], F32R, o)
        rch, o = place("rch", [RW, 8], F32R, o)
        rcl, o = place("rcl", [RW, 8], F32, o)
        sd, o = place("sd", [RW, 8], F32, o)
        rc, o = place("rc", [RW, 8], F32, o)
        par, o = place("par", [P, NPAR], F32, o)
        con, o = place("con", [P, 3 * P], F32, o)
        lam, o = place("lam", [P, 8], F32, o)
        negA, o = place("negA", [HEADS, 8], F32, o)
        h, o = place("h", [P, KT, T], F32, o)
        oh = o - 4 * KT * T
        phase = o

        ones = con[:, K_ONES:K_ONES + P]
        ident = con[:, K_ID:K_ID + P]
        mask = con[:, K_MASK:K_MASK + P]

        cv, _ = place("cv", [P, 2, 4, T], F32, oh)
        part, _ = place("part", [P, KT, T], F32, 0)
        o = phase
        yh, o = place("yh", [P, 2 * G, T], F32R, o)
        yl0 = o
        yl, o = place("yl", [P, 2 * G, T], F32R, o)
        dt_tmp, _ = place("dt_tmp", [HEADS, 10, T], F32, yl0 + 4 * T * 6)
        cong, _ = place("cong", [BUCKETS, 2 * ND], F32, phase + 4 * T * 6)
        gvec, _ = place("gvec", [AH, ND], F32, phase + 4 * T * 12)
        rb0, o = place("rb0", [P, T], F32, o)
        rawc, o = place("rawc", [P, T + TAPS - 1], F32, o)
        th, o = place("th", [P, T], F32, o)
        zth, o = place("zth", [P, T], F32, o)
        zs, o = place("zs", [P, 2, 2, T], F32, o)
        ybuf, o = place("ybuf", [P, 2, T], F32, o)
        y2, o = place("y2", [P, 2, T], F32, o)
        bc, o = place("bc", [P, 2, 2, HPG, P], F32, o)
        Lm, o = place("Lm", [P, 2, HPG, P], F32, o)
        Cs, o = place("Cs", [P, 2, HPG, P], F32, o)
        xdt, o = place("xdt", [P, 2, HPG * 64], F32, o)
        xst, o = place("xst", [P, 2, HPG * 64], F32, o)
        dend, o = place("dend", [P, 2, HPG], F32, o)
        Btok, o = place("Btok", [P, 2, P], F32, o)
        cbm, o = place("cbm", [P, 2, P], F32, o)
        state, o = place("state", [P, HPG * 64], F32, o)
        stmp, o = place("stmp", [P, HPG * 64], F32, o)
        tok, o = place("tok", [P, NC, 3, HEADS], F32, o)
        decg, o = place("decg", [P, 2, NC, HPG], F32, o)

        o = phase
        hh, o = place("hh", [P, FT, T], F32R, o)
        hl, o = place("hl", [P, FT, T], F32R, o)
        gb, o = place("gb", [P, 3, T], F32, o)
        vb, o = place("vb", [P, 3, T], F32, o)

        o = phase
        kh, o = place("kh", [P, KT, T], F32R, o)
        kl, o = place("kl", [P, KT, T], F32R, o)
        oTh, o = place("oTh", [P, AH, T], F32R, o)
        oTl, o = place("oTl", [P, AH, T], F32R, o)
        kT, o = place("kT", [P, 2, T], F32, o)
        qT, o = place("qT", [P, 2, T], F32, o)
        qTh, o = place("qTh", [P, 2, T], F32R, o)
        qTl, o = place("qTl", [P, 2, T], F32R, o)
        kTh, o = place("kTh", [P, 2, T], F32R, o)
        kTl, o = place("kTl", [P, 2, T], F32R, o)
        vT, o = place("vT", [P, T], F32, o)
        vtok, o = place("vtok", [P, NC, P], F32, o)
        bias, o = place("bias", [P, 2, T], F32, o)
        pr, o = place("pr", [P, 2, 2, T], F32, o)
        aT, o = place("aT", [P, 2, NC, P], F32, o)
        oraw, o = place("oraw", [P, 2, T], F32, o)
        on, o = place("on", [P, T], F32, o)
        rb2, o = place("rb2", [P, T], F32, o)
        sm, o = place("sm", [P, 2, 9], F32, o)

        acc = [ctx.enter_context(nc.psum_tensor(f"acc{p}", [P, 2, 512], F32)) for p in range(2)]
        psAY = ctx.enter_context(nc.psum_tensor("psAY", [P, 2, 512], F32))
        psA, psY = psAY[:, 0, :], psAY[:, 1, :]
        psS = ctx.enter_context(nc.psum_tensor("psS", [P, 512], F32))
        psF = ctx.enter_context(nc.psum_tensor("psF", [P, 512], F32))

        scr = nc.dram_tensor("scr_acs", [2, HEADS, T], F32, kind="Internal").ap()
        scr_b = nc.dram_tensor("scr_bias", [AH, P * ND], F32, kind="Internal").ap()

        raw_in = [sem(f"raw_in{s}") for s in range(3)]
        hi_ready = sem("hi_ready")
        lo_ready = sem("lo_ready")
        unit_done = sem("unit_done")
        acc_free = [sem("acc_free0"), sem("acc_free1")]
        par_in, con_in, cong_in = sem("par_in"), sem("con_in"), sem("cong_in")
        x_sem = [sem(f"x_in{q}") for q in range(4)]
        sq_done, ssq_done, ssq_zero = sem("sq_done"), sem("ssq_done"), sem("ssq_zero")
        n_stat, n_sd, n_rc, n_diag = sem("n_stat"), sem("n_sd"), sem("n_rc"), sem("n_diag")
        n_bc, n_rb = sem("n_bc"), sem("n_rb")
        decg_done = sem("decg_done")
        u_hi, u_lo = sem("u_hi"), sem("u_lo")
        setup = sem("setup")
        lam_mm, lam_exp, hot_mm, gvec_out = sem("lam_mm"), sem("lam_exp"), sem("hot_mm"), sem("gvec_out")
        dt_x, dt_v, dt_a, tok_t, tok_ready, scr_out = (
            sem("dt_x"), sem("dt_v"), sem("dt_a"), sem("tok_t"), sem("tok_ready"), sem("scr_out"))
        tap3_done, tap2_done, tap1_done, taps_done = (
            sem("tap3_done"), sem("tap2_done"), sem("tap1_done"), sem("taps_done"))
        tanh_done, conv_ready, ztanh_done, z_done = (
            sem("tanh_done"), sem("conv_ready"), sem("ztanh_done"), sem("z_done"))
        bc_in = [sem("bc_in0"), sem("bc_in1")]
        chunk_t, xdt_done, cbm_done, seg_done, exp_done, wt_done = (
            sem("chunk_t"), sem("xdt_done"), sem("cbm_done"), sem("seg_done"), sem("exp_done"), sem("wt_done"))
        xst_done, cs_done, scan_done, stmp_done, st_done, yadd_done = (
            sem("xst_done"), sem("cs_done"), sem("scan_done"), sem("stmp_done"), sem("st_done"), sem("yadd_done"))
        y2_done, f_sq, f_sum, f_stat, f_sd, f_rc, f_diag, f_bc, f_rb, f_yn, f_hi, f_lo = (
            sem("y2_done"), sem("f_sq"), sem("f_sum"),
            sem("f_stat"), sem("f_sd"), sem("f_rc"), sem("f_diag"), sem("f_bc"),
            sem("f_rb"), sem("f_yn"), sem("f_hi"), sem("f_lo"))
        part_in = sem("part_in")
        k_hi, k_lo = sem("k_hi"), sem("k_lo")
        bias_in = [sem("bias_in0"), sem("bias_in1")]
        v_t, v_tok, s_mm, s_max, p_exp, p_rec, p_lam, p_half, p_comb = (
            sem("v_t"), sem("v_tok"), sem("s_mm"), sem("s_max"), sem("p_exp"), sem("p_rec"), sem("p_lam"),
            sem("p_half"), sem("p_comb"))
        qk_hi, qk_lo = sem("qk_hi"), sem("qk_lo")
        p_t, p_tc, o_mm, o_out, o2_mm = sem("p_t"), sem("p_tc"), sem("o_mm"), sem("o_out"), sem("o2_mm")
        h_sq, h_stat, h_sd, h_rc, h_diag, h_bc, h_rb, h_on, h_hi, h_lo = (
            sem("h_sq"), sem("h_stat"), sem("h_sd"), sem("h_rc"), sem("h_diag"), sem("h_bc"), sem("h_rb"),
            sem("h_on"), sem("h_hi"), sem("h_lo"))
        silu_done, hid_done, hid_hi, hid_lo = sem("silu_done"), sem("hid_done"), sem("hid_hi"), sem("hid_lo")
        ones_done = sem("ones_done")
        hw_done, out_f, out_p, stored = sem("hw_done"), sem("out_f"), sem("out_p"), sem("stored")

        block = ctx.enter_context(nc.Block())

        class Idx:

            def __init__(self, first, rate=0, turn=0):
                self.first, self.rate, self.turn = first, rate, turn

            def __add__(self, k):
                return Idx(self.first + k, self.rate, self.turn)

            def mul(self, k, plus=0):
                return self.turn * (self.rate * k) + (self.first * k + plus) if self.rate else self.first * k + plus

            @property
            def v(self):
                return self.mul(1)

            def times(self, k, plus=0):
                return Idx(self.first * k + plus, self.rate * k, self.turn)

            def div(self, m):
                assert self.rate % m == 0
                return Idx(self.first // m, self.rate // m, self.turn)

        def load_unit(e, u):
            s = u.first % 3
            if later((u + -2).v):
                e.wait_ge(lo_ready, (u + -2).v)
            e.dma_start(raw[s][:].rearrange("p k c -> p (k c)"),
                        w_all[at(u.v)].rearrange("a p f -> p (a f)")).then_inc(raw_in[s], 16)

        def split_hi(e, u):
            s = u.first % 3
            e.wait_ge(raw_in[s], u.div(3).mul(16, 16))
            if later((u + -2).v):
                e.wait_ge(unit_done, (u + -2).v)
            e.activation(wh[s][:], raw[s][:], ACT.Copy).then_inc(hi_ready, 1)

        def split_lo(e, u):
            s = u.first % 3
            e.wait_ge(hi_ready, (u + 1).v)
            e.tensor_tensor(wl[s][:], raw[s][:], wh[s][:].bitcast(F32), ALU.subtract).then_inc(lo_ready, 1)

        def look_ahead(e, split, u):
            if u.rate or u.first + 3 < UNITS:
                split(e, u + 3)

        def multiply(e, u, n, xh, xl, k0=0, ks=KT, first=True, last=True, slices=None, moving=None):
            s, a = u.first % 3, acc[n.first % 2]
            for k in (range(ks) if slices is None else slices):
                if k == 0:
                    e.wait_ge(lo_ready, (u + 1).v)
                    if first:
                        if later(n.div(2).v):
                            e.wait_ge(acc_free[n.first % 2], n.div(2).v)
                if moving:
                    e.wait_ge(moving[0], moving[1] + k + 1)
                for i, (wt, mv) in enumerate(((wh, xh), (wh, xl), (wl, xh))):
                    for half in range(2):
                        mm = e.matmul(a[:, half, 0:H2], wt[s][:, k, :], mv[:, k0 + k, H2 * half:H2 * half + H2],
                                      start=(first and k == 0 and i == 0), stop=(last and k == ks - 1 and i == 2))
                if k == ks - 1:
                    mm.then_inc(unit_done, 1)

        def halves(t):
            return t.rearrange("p (a b) -> p a b", a=2)

        def tile_of(t, m):
            return t[:, at(m.v), :].rearrange("p a t -> p (a t)")

        def taken(e, n):
            e.wait_ge(acc_free[n.first % 2], n.div(2).mul(1, 1))

        def acc_of(n):
            return acc[n.first % 2][:, :, 0:H2]

        def free(ins, n):
            ins.then_inc(acc_free[n.first % 2], 1)

        def stats(e, src, n_src, at_col=0):
            for t in range(NR):
                for j in range(n_src):
                    mm = e.matmul(psF[0:RW, at_col + t:at_col + t + 1], src[:, j, RW * t:RW * t + RW], ones[:, 0:1],
                                  start=(j == 0), stop=(j == n_src - 1))
            return mm

        def reciprocals(e, sd_sem, rc_sem, i):
            e.wait_ge(sd_sem, i.mul(1, 1))
            e.reciprocal(rc[0:RW, 0:NR], sd[0:RW, 0:NR]).then_inc(rc_sem, 1)
            e.wait_ge(rc_sem, i.mul(3, 1))
            e.tensor_copy(rch[0:RW, 0:NR], rc[0:RW, 0:NR]).then_inc(rc_sem, 1)
            e.wait_ge(rc_sem, i.mul(3, 2))
            e.tensor_tensor(rcl[0:RW, 0:NR], rc[0:RW, 0:NR], rch[0:RW, 0:NR].bitcast(F32),
                            ALU.subtract).then_inc(rc_sem, 1)

        def on_diagonal(e, rc_sem, dg_sem, i):
            eye = ident[0:RW, 0:RW].unsqueeze(1).broadcast_to((RW, NR, RW))
            e.wait_ge(rc_sem, i.mul(3, 3))
            e.tensor_tensor(diagh[:], eye, rch[0:RW, 0:NR].bitcast(F32).unsqueeze(2).broadcast_to((RW, NR, RW)),
                            ALU.mult)
            e.tensor_tensor(diagl[:], eye, rcl[0:RW, 0:NR].unsqueeze(2).broadcast_to((RW, NR, RW)),
                            ALU.mult).then_inc(dg_sem, 1)

        def spread(e, half, psum):
            e.matmul(psum[:, 0:H2], ones_r[0:RW, :], diagh[:, 3 * half:3 * half + 3, :], start=True, stop=False)
            return e.matmul(psum[:, 0:H2], ones_r[0:RW, :], diagl[:, 3 * half:3 * half + 3, :], start=False, stop=True)

        def norm_stats_pe(e, i):
            e.wait_ge(ssq_done, KT * (i + 1))
            stats(e, ssq[:].unsqueeze(1), 1).then_inc(n_stat, 1)

        def norm_spread_pe(e, i):
            e.wait_ge(n_diag, i + 1)
            spread(e, 0, psA)
            spread(e, 1, psY).then_inc(n_bc, 1)

        def norm_act(e, i):
            e.wait_ge(n_stat, i + 1)
            e.activation(sd[0:RW, 0:NR], psF[0:RW, 0:NR], ACT.Sqrt, scale=1.0 / D,
                         bias=par[0:RW, C_EPS:C_EPS + 1]).then_inc(n_sd, 1)
            e.wait_ge(n_bc, i + 1)
            dst = rb if i else rb0
            e.activation(dst[:, 0:H2], psA[:, 0:H2], ACT.Copy)
            e.activation(dst[:, H2:T], psY[:, 0:H2], ACT.Copy).then_inc(n_rb, 1)

        def norm_dve(e, i):
            reciprocals(e, n_sd, n_rc, Idx(i))
            on_diagonal(e, n_rc, n_diag, Idx(i))
            if i < 4:
                e.wait_ge(n_stat, i + 1)
                e.memset(ssq[:], 0.0).then_inc(ssq_zero, 1)

        def square(e, idx, slot, tile):
            if later((idx + -1).v):
                e.wait_ge(ssq_done, (idx + -1).v)
            e.activation(sqt[:, slot, :], tile, ACT.Square).then_inc(sq_done, 1)

        def add_squares(e, idx, slot):
            e.wait_ge(sq_done, (idx + 1).v)
            if later(idx.v):
                e.wait_ge(ssq_done, idx.v)
            e.tensor_tensor(ssq[:], ssq[:], sqt[:, slot, :], ALU.add).then_inc(ssq_done, 1)

        def residual_act(e, n, m, slot, i, w):
            taken(e, n)
            square(e, m + KT * i, slot, tile_of(h, m))
            if w is not None:
                e.activation(tile_of(uh, m),
                             tile_of(h, m), ACT.Identity,
                             scale=par[:, at((m + C_NORM + 8 * w).v)]).then_inc(u_hi, 1)

        def residual_dve(e, n, done, m, slot, i, w, base):
            take_residual(e, n, done, m, base)
            rest_of_residual(e, m, slot, i, w)

        def take_residual(e, n, done, m, base):
            e.wait_ge(*done)
            free(e.tensor_tensor(halves(tile_of(h, m)), acc_of(n), halves(tile_of(base, m)), ALU.add), n)

        def rest_of_residual(e, m, slot, i, w):
            add_squares(e, m + KT * i, slot)
            if w is not None:
                e.wait_ge(u_hi, (m + KT * i + 1).v)
                e.scalar_tensor_tensor(out=tile_of(ul, m), in0=tile_of(h, m),
                                       scalar=par[:, at((m + C_NORM + 8 * w).v)],
                                       in1=tile_of(uh, m).bitcast(F32),
                                       op0=ALU.mult, op1=ALU.subtract).then_inc(u_lo, 1)

        def down_turns(e, tile, between=None):
            with e.Fori(0, 3) as i:
                for q in range(2):
                    tile(e, Idx(3 * q, 6, i), Idx(q, 2, i), q)
            if between:
                between(e)
            for q in range(2):
                tile(e, Idx(18 + 3 * q), Idx(6 + q), q)

        def pair_turns(e, pair):
            with e.Fori(0, 7) as i:
                for q in range(3):
                    pair(e, Idx(2 + 2 * q, 6, i), Idx(1 + q, 3, i), (1 + q) % 3)

        @block.sync
        def _(sp):
            sp.dma_start(par[:], par_d).then_inc(par_in, 16)
            load_unit(sp, Idx(0))
            for q in range(4):
                sp.dma_start(h[:, 2 * q:2 * q + 2, :], x_t[:, 2 * q:2 * q + 2, :]).then_inc(x_sem[q], 16)
            sp.dma_start(con[:], con_d[:, 0:3 * P]).then_inc(con_in, 16)
            load_unit(sp, Idx(1))
            load_unit(sp, Idx(2))
            sp.dma_start(cong[:], con_d[0:BUCKETS, K_HOT:NCON]).then_inc(cong_in, 16)
            turns = (UNITS - 3) // 3
            with sp.Fori(0, turns) as i:
                for s in range(3):
                    load_unit(sp, Idx(3 + s, 3, i))
            for u in range(3 + 3 * turns, UNITS):
                load_unit(sp, Idx(u))
            for first, tiles, ready, count in ((POOLED, 2, out_f, 2), (POOLED + 2, 2, out_f, 4),
                                               (0, POOLED, out_p, POOLED), (POOLED + 4, 1, out_f, 5)):
                sp.wait_ge(ready, count)
                sp.dma_start(out_d[:, first:first + tiles, :], h[:, first:first + tiles, META:T]).then_inc(stored, 16)
            sp.wait_ge(stored, 64)

        def u_in(k, j):
            return k.times(6, U_IN + j)

        def n_in(k, j):
            return k.times(6, N_IN + j)

        def ssd_steps(e, step, between=None):
            step(e, Idx(0), 0, "in", False, False)
            step(e, Idx(1), 1, "in", True, False)
            with e.Fori(0, 3) as i:
                step(e, Idx(2, 2, i), 0, "in", True, True)
                step(e, Idx(3, 2, i), 1, "in", True, True)
            if between:
                between(e)
            step(e, Idx(8), 0, "out", True, True)
            step(e, Idx(9), 1, "out", False, True)

        def out1(k, j):
            m = 6 * (k.first - 8) + j
            return m if m < KT else None

        S_X, S_E, S_S, S_Q, S_P, S_DT, S_ACS, S_DEC, S_DA, S_EXP = range(10)

        def pe_chunk_in(e, g, gp, c):
            t0, q = CH[c]
            if c == 0:
                e.wait_ge(conv_ready, g.mul(4, 4))
            if later(g.mul(NC, c)):
                e.wait_ge(cbm_done, g.mul(NC, c))
            for j, t in enumerate((2, 3, 1)):
                e.transpose(psA[0:q, P * j:P * j + P], cv[:, gp, t, t0:t0 + q], ident)
            e.matmul(psA[0:q, 3 * P:3 * P + q], cv[:, gp, 1, t0:t0 + q], cv[:, gp, 0, t0:t0 + q],
                     start=True, stop=True).then_inc(chunk_t, 1)

        def pe_chunk_out(e, g, gp, c):
            t0, q = CH[c]
            b = (gp + c) % 2
            e.wait_ge(wt_done, g.mul(NC, c + 1))
            e.wait_ge(xst_done, g.mul(NC, c + 1))
            if later(g.mul(NC, c)):
                e.wait_ge(yadd_done, g.mul(NC, c))
            if c:
                e.wait_ge(cs_done, g.mul(NC - 1, c))
                e.wait_ge(st_done, g.mul(NC - 1, c))
            for r in range(HPG):
                dst = psY[64 * (r % 2):64 * (r % 2) + 64, P * (r // 2):P * (r // 2) + q]
                mm = e.matmul(dst, xdt[0:q, b, 64 * r:64 * r + 64], Lm[0:q, b, r, 0:q], start=True, stop=(c == 0))
                if c:
                    mm = e.matmul(dst, state[:, 64 * r:64 * r + 64], Cs[:, b, r, 0:q], start=False, stop=True)
            if c < NC - 1:
                mm = e.matmul(psS[:, 0:HPG * 64], Btok[0:q, b, :], xst[0:q, b, :], start=True, stop=True)
            mm.then_inc(scan_done, 1)

        def dt_token_major(e):
            e.wait_ge(dt_a, 7)
            e.wait_ge(dt_v, DT_STEPS)
            for c, (t0, q) in enumerate(CH):
                for i, src in enumerate((S_ACS, S_DT, S_DEC)):
                    mm = e.transpose(psF[0:q, (3 * c + i) * HEADS:(3 * c + i + 1) * HEADS],
                                     dt_tmp[:, src, t0:t0 + q], ident[0:HEADS, 0:HEADS])
            mm.then_inc(tok_t, 1)

        def beside_last_norm(e, j):
            if j == 3:
                e.wait_ge(f_lo, 1 + G - 1)
            plan = {3: [(0, range(3))], 4: [(0, range(3, 4))], 5: [(0, range(4, 6)), (1, range(6))]}
            for m, slices in plan.get(j, []):
                multiply(e, Idx(U_OUT2 + m), Idx(N_OUT2 + m), yh[:, KT:, :], yl[:, KT:, :], slices=slices)

        def pe_step(e, k, kp, units, ssd, fin):
            g, gp, f = k + -1, 1 - kp, k + -2
            for j in range(6):
                if units == "in" and (k.rate or k.first or j):
                    multiply(e, u_in(k, j), n_in(k, j), uh, ul)
                elif units == "out" and out1(k, j) is not None:
                    m = out1(k, j)
                    if m == 0:
                        e.wait_ge(f_lo, 1 + 4)
                    multiply(e, Idx(U_OUT1 + m), Idx(N_OUT1 + m), yh, yl)
                if k.first == 9:
                    beside_last_norm(e, j)
                if fin and j == 2:
                    e.wait_ge(f_sum, f.mul(1, 1))
                    stats(e, sqt[:, 0:1, :], 1).then_inc(f_stat, 1)
                if fin and j in (3, 4):
                    e.wait_ge(f_diag, f.mul(1, 1))
                    if j == 4:
                        e.wait_ge(f_rb, f.mul(2, 1))
                    spread(e, j - 3, psF).then_inc(f_bc, 1)
                if k.first == 1 and j == 0:
                    dt_token_major(e)
                    e.wait_ge(setup, 7)
                if ssd and j < NC:
                    pe_chunk_in(e, g, gp, j)
                if ssd and j >= 1:
                    pe_chunk_out(e, g, gp, j - 1)

        def gate_squares(e, f):
            e.wait_ge(y2_done, f.mul(1, 1))
            e.activation(sqt[:], y2[:], ACT.Square).then_inc(f_sq, 1)

        def gate_sd(e, f):
            e.wait_ge(f_stat, f.mul(1, 1))
            e.activation(sd[0:RW, 0:NR], psF[0:RW, 0:NR], ACT.Sqrt, scale=1.0 / (2 * P),
                         bias=par[0:RW, C_EPS + 1:C_EPS + 2]).then_inc(f_sd, 1)

        def act_step(e, k, kp, units, ssd, fin):
            g, gp, f = k + -1, 1 - kp, k + -2
            for j in range(6):
                if k.first == 9 and j == 0:
                    gate_squares(e, f)
                if k.first == 1 and j == 0:
                    e.wait_ge(scr_out, 32)
                    load_decay(e, Idx(0), 0, 0)
                if ssd and j < NC - 1:
                    load_decay(e, g, gp, j + 1)
                if ssd and j == NC - 1 and units == "in":
                    load_decay(e, g + 1, kp, 0)
                if units == "in":
                    u, n = u_in(k, j), n_in(k, j)
                    if 1 <= j <= 4:
                        if later(k.mul(4, j)):
                            e.wait_ge(taps_done, k.mul(4, j))
                        if later(k.mul(4, j - 1)):
                            e.wait_ge(conv_ready, k.mul(4, j - 1))
                        e.activation(th[:], cv[:, kp, j - 1, :], ACT.Tanh).then_inc(tanh_done, 1)
                    if j < 4:
                        taken(e, n)
                        if later((k + -1).mul(NC)):
                            e.wait_ge(yadd_done, (k + -1).mul(NC))
                        if later((k + -1).mul(NC - 1)):
                            e.wait_ge(cs_done, (k + -1).mul(NC - 1))
                        col = k.mul(20, C_CONV + 5 * j)
                        e.activation(cv[:, kp, j, :], rawc[:, TAPS - 1:], ACT.Identity,
                                     scale=par[:, at(col + 3)], bias=par[:, at(col + 4)]).then_inc(tap3_done, 1)
                    else:
                        taken(e, n)
                        if later(k.mul(2, j - 4)):
                            e.wait_ge(z_done, k.mul(2, j - 4))
                        e.activation(zth[:], zs[:, kp, j - 4, :], ACT.Tanh, scale=0.5).then_inc(ztanh_done, 1)
                    if fin and j == 2:
                        gate_sd(e, f)
                    e.wait_ge(unit_done, (u + 1).v)
                    look_ahead(e, split_hi, u)
                else:
                    if fin and j == 2:
                        gate_sd(e, f)
                    if out1(k, j) is not None:
                        look_ahead(e, split_hi, Idx(U_OUT1 + out1(k, j)))
                if ssd and j < NC:
                    q, b = CH[j][1], (gp + j) % 2
                    e.wait_ge(seg_done, g.mul(NC, j + 1))
                    e.activation(Lm[0:q, b, :, 0:q], Lm[0:q, b, :, 0:q], ACT.Exp).then_inc(exp_done, 1)
                if fin and j == 1 and k.first < 9:
                    gate_squares(e, f)
                if fin and j in (3, 4):
                    e.wait_ge(f_bc, f.mul(2, j - 2))
                    e.activation(rb[:, H2 * (j - 3):H2 * (j - 2)], psF[:, 0:H2], ACT.Copy).then_inc(f_rb, 1)
                if fin and j == 5:
                    e.wait_ge(f_yn, f.mul(2, 2))
                    e.activation(yh[:, at(f.mul(2), 2), :], y2[:], ACT.Copy).then_inc(f_hi, 1)
                if k.rate == 0 and k.first == 0 and j == 1:
                    e.wait_ge(lam_mm, 1)
                    e.activation(lam[:, 2:4], psS[:, 0:2], ACT.Exp).then_inc(lam_exp, 1)
                if k.first == 1 and j == 0:
                    e.wait_ge(setup, 7)
                    e.dma_start(scr_b.rearrange("h (p m) -> h p m", m=ND),
                                gvec[:].unsqueeze(1).broadcast_to((AH, P, ND))).then_inc(gvec_out, 16)
                if k.rate == 0 and k.first == 0 and j == 5:
                    dt_tables_act(e)

        def load_decay(e, g, gp, c):
            t0, q = CH[c]
            b = (gp + c) % 2
            s = g.times(NC, c)
            if later((s + -1).v):
                e.wait_ge(seg_done, (s + -1).v)
            if later(g.mul(NC - 1, (-1, 0, 0, 1, 2)[c])):
                e.wait_ge(cs_done, g.mul(NC - 1, (-1, 0, 0, 1, 2)[c]))
            for i in range(2):
                src = scr[i, at(g.mul(HPG), HPG), t0:t0 + q]
                e.dma_start(bc[:, b, i, :, 0:q], src.unsqueeze(0).broadcast_to((P, HPG, q))).then_inc(bc_in[b], 16)

        def decay_in(e, g, c, b):
            e.wait_ge(bc_in[b], g.times(NC, c).div(2).mul(32, 32))

        def dve_step(e, k, kp, units, ssd, fin):
            g, gp, f = k + -1, 1 - kp, k + -2
            for j in range(6):
                if fin and j == 0:
                    e.wait_ge(yadd_done, f.mul(NC, NC))
                    e.wait_ge(f_lo, f.mul(1, 1))
                    e.tensor_tensor(y2[:], ybuf[:], zs[:, kp], ALU.mult).then_inc(y2_done, 1)
                if units == "in":
                    n = n_in(k, j)
                    e.wait_ge(unit_done, (u_in(k, j) + 1).v)
                    if j < 4:
                        if later(k.mul(4, j)):
                            e.wait_ge(taps_done, k.mul(4, j))
                        free(e.tensor_tensor(halves(rawc[:, TAPS - 1:]), acc_of(n), halves(rb0[:]), ALU.mult), n)
                    else:
                        if later((k + -1).v):
                            e.wait_ge(y2_done, (k + -1).v)
                        free(e.tensor_tensor(halves(zs[:, kp, j - 4, :]), acc_of(n), halves(rb0[:]), ALU.mult), n)
                if k.first == 1 and j == 0:
                    e.wait_ge(tok_t, 1)
                    e.tensor_copy(tok[0:META, 0, :, :], psF[0:META, 0:3 * HEADS].rearrange("p (i h) -> p i h", i=3))
                    e.tensor_copy(tok[:, 1:NC, :, :],
                                  psF[:, 3 * HEADS:3 * NC * HEADS].rearrange("p (c i h) -> p c i h", i=3, h=HEADS)
                                  ).then_inc(tok_ready, 1)
                    e.wait_ge(tok_ready, 1)
                if ssd and j < NC:
                    t0, q = CH[j]
                    b = (gp + j) % 2
                    heads = at(g.mul(HPG), HPG)
                    e.wait_ge(chunk_t, g.mul(NC, j + 1))
                    if later(g.mul(NC, j - 1)):
                        e.wait_ge(scan_done, g.mul(NC, j - 1))
                    e.tensor_tensor(xdt[0:q, b, :].rearrange("p (r c) -> p r c", r=HPG),
                                    psA[0:q, 0:2 * P].rearrange("p (r c) -> p r c", r=HPG),
                                    tok[0:q, j, 1, heads].unsqueeze(2).broadcast_to((q, HPG, 64)),
                                    ALU.mult).then_inc(xdt_done, 1)
                    e.tensor_copy(Btok[0:q, b, :], psA[0:q, 2 * P:3 * P])
                    e.tensor_tensor(cbm[0:q, b, 0:q], psA[0:q, 3 * P:3 * P + q], mask[0:q, 0:q],
                                    ALU.mult).then_inc(cbm_done, 1)
                    decay_in(e, g, j, b)
                    if 1 <= j < NC - 1:
                        e.tensor_copy(dend[:, b, :], bc[:, b, 1, :, q - 1])
                    for r in range(HPG):
                        ins = e.tensor_scalar(Lm[0:q, b, r, 0:q], bc[0:q, b, 0, r, 0:q],
                                              tok[0:q, j, 0, at(g.mul(HPG, r))], 0.0, ALU.subtract, ALU.min)
                    ins.then_inc(seg_done, 1)
                if fin and j == 2:
                    reciprocals(e, f_sd, f_rc, f)
                    if k.first == 9:
                        on_diagonal(e, f_rc, f_diag, f)
                if units == "in" and 1 <= j <= 4:
                    e.wait_ge(tanh_done, k.mul(4, j))
                    e.scalar_tensor_tensor(out=cv[:, kp, j - 1, :], in0=th[:], scalar=1.0, in1=cv[:, kp, j - 1, :],
                                           op0=ALU.add, op1=ALU.mult).then_inc(conv_ready, 1)
                if units == "in":
                    if j < 4:
                        for tap, before, after in ((2, tap3_done, tap2_done), (1, tap2_done, tap1_done),
                                                   (0, tap1_done, taps_done)):
                            e.wait_ge(before, k.mul(4, j + 1))
                            e.scalar_tensor_tensor(out=cv[:, kp, j, :], in0=rawc[:, tap:tap + T],
                                                   scalar=par[:, at(k.mul(20, C_CONV + 5 * j + tap))],
                                                   in1=cv[:, kp, j, :], op0=ALU.mult, op1=ALU.add
                                                   ).then_inc(after, 1)
                elif out1(k, j) is not None:
                    m = out1(k, j)
                    e.wait_ge(part_in, 16)
                    e.wait_ge(unit_done, U_OUT1 + m + 1)
                    free(e.tensor_tensor(halves(part[:, m, :]), acc_of(Idx(N_OUT1 + m)), halves(part[:, m, :]),
                                         ALU.add), Idx(N_OUT1 + m))
                if ssd and j >= 1:
                    c = j - 1
                    t0, q = CH[c]
                    b = (gp + c) % 2
                    e.wait_ge(scan_done, g.mul(NC, c + 1))
                    if c == 0:
                        e.tensor_copy(state[:], psS[:, 0:HPG * 64]).then_inc(st_done, 1)
                    elif c < NC - 1:
                        e.wait_ge(st_done, g.mul(NC - 1, c))
                        e.tensor_tensor(stmp[:].rearrange("p (r c) -> p r c", r=HPG),
                                        state[:].rearrange("p (r c) -> p r c", r=HPG),
                                        dend[:, b, :].unsqueeze(2).broadcast_to((P, HPG, 64)),
                                        ALU.mult).then_inc(stmp_done, 1)
                        e.wait_ge(stmp_done, g.mul(NC - 2, c))
                        e.tensor_tensor(state[:], psS[:, 0:HPG * 64], stmp[:], ALU.add).then_inc(st_done, 1)
                    if c == 0:
                        if later(g.v):
                            e.wait_ge(y2_done, g.v)
                    for i in range(2):
                        ins = e.scalar_tensor_tensor(out=ybuf[:, i, t0:t0 + q], in0=cv[:, gp, 2 + i, t0:t0 + q],
                                                     scalar=par[:, at(g.mul(2, C_DSKIP + i))],
                                                     in1=psY[:, P * i:P * i + q], op0=ALU.mult, op1=ALU.add)
                    ins.then_inc(yadd_done, 1)
                if units == "in" and j >= 4:
                    e.wait_ge(ztanh_done, k.mul(2, j - 3))
                    e.scalar_tensor_tensor(out=zs[:, kp, j - 4, :], in0=zth[:], scalar=1.0, in1=zs[:, kp, j - 4, :],
                                           op0=ALU.add, op1=ALU.mult).then_inc(z_done, 1)
                if ssd and j < NC:
                    q, b = CH[j][1], (gp + j) % 2
                    e.wait_ge(exp_done, g.mul(NC, j + 1))
                    e.wait_ge(cbm_done, g.mul(NC, j + 1))
                    e.tensor_tensor(Lm[0:q, b, :, 0:q], Lm[0:q, b, :, 0:q],
                                    cbm[0:q, b, 0:q].unsqueeze(1).broadcast_to((q, HPG, q)),
                                    ALU.mult).then_inc(wt_done, 1)
                if fin and j == 5:
                    e.wait_ge(f_rb, f.mul(2, 2))
                    for i in range(2):
                        e.scalar_tensor_tensor(out=y2[:, i, :], in0=y2[:, i, :],
                                               scalar=par[:, at(f.mul(2, C_SSMN + i))], in1=rb[:],
                                               op0=ALU.mult, op1=ALU.mult).then_inc(f_yn, 1)
                    e.wait_ge(f_hi, f.mul(1, 1))
                    e.tensor_tensor(yl[:, at(f.mul(2), 2), :], y2[:],
                                    yh[:, at(f.mul(2), 2), :].bitcast(F32), ALU.subtract).then_inc(f_lo, 1)
                if k.rate == 0 and k.first == 0 and j < 5:
                    dt_second(e, j)
                if k.rate == 0 and k.first == 0 and j == 5:
                    attention_constants(e)

        def dt_first(e):
            t = lambda i: dt_tmp[:, i, :]
            e.wait_ge(unit_done, 1)
            free(e.tensor_tensor(halves(t(S_Q)), acc[0][0:HEADS, :, 0:H2], halves(rb0[0:HEADS, :]),
                                 ALU.mult), Idx(0))
            taken(e, Idx(0))
            e.tensor_scalar(t(S_X), t(S_Q), par[0:HEADS, C_DTB:C_DTB + 1], None, ALU.add).then_inc(dt_x, 1)
            e.wait_ge(dt_x, 1)
            e.scalar_tensor_tensor(out=t(S_E), in0=t(S_X), scalar=-1.0, in1=t(S_X), op0=ALU.mult,
                                   op1=ALU.min).then_inc(dt_v, 1)
            e.wait_ge(dt_a, 2)
            e.tensor_scalar(t(S_S), t(S_E), 2.0, None, ALU.add).then_inc(dt_v, 1)
            e.wait_ge(dt_v, 2)
            e.reciprocal(t(S_Q), t(S_S)).then_inc(dt_v, 1)
            e.wait_ge(dt_v, 3)
            e.tensor_tensor(t(S_S), t(S_E), t(S_Q), ALU.mult).then_inc(dt_v, 1)
            e.wait_ge(dt_v, 4)
            e.tensor_tensor(t(S_Q), t(S_S), t(S_S), ALU.mult).then_inc(dt_v, 1)
            e.wait_ge(dt_v, 5)
            e.tensor_scalar(t(S_P), t(S_Q), ATANH[0], None, ALU.mult).then_inc(dt_v, 1)

        def attention_constants(e):
            e.wait_ge(lam_exp, 1)
            e.tensor_tensor(lam[:, 4:5], lam[:, 3:4], lam[:, 2:3], ALU.subtract).then_inc(setup, 1)
            e.wait_ge(setup, 4)
            e.tensor_scalar(lam[:, 5:6], lam[:, 4:5], -LAMBDA_INIT, None, ALU.add).then_inc(setup, 1)
            e.wait_ge(hot_mm, 1)
            e.scalar_tensor_tensor(out=gvec[:, 0:512], in0=psA[0:AH, 0:512], scalar=-1.0,
                                     in1=cong[0:AH, ND:ND + 512], op0=ALU.mult, op1=ALU.add).then_inc(setup, 1)
            e.scalar_tensor_tensor(out=gvec[:, 512:ND], in0=psY[0:AH, 0:ND - 512], scalar=-1.0,
                                     in1=cong[0:AH, ND + 512:2 * ND], op0=ALU.mult, op1=ALU.add).then_inc(setup, 1)

        def dt_second(e, part):
            t = lambda i: dt_tmp[:, i, :]
            for x, c in enumerate(ATANH[1:]):
                if x // 2 == part:
                    e.wait_ge(dt_v, 6 + x)
                    e.scalar_tensor_tensor(out=t(S_P), in0=t(S_P), scalar=c, in1=t(S_Q), op0=ALU.add,
                                           op1=ALU.mult).then_inc(dt_v, 1)
            done = 5 + len(ATANH)
            if part == 3:
                e.wait_ge(dt_v, done)
                e.scalar_tensor_tensor(out=t(S_P), in0=t(S_P), scalar=1.0, in1=t(S_S), op0=ALU.add,
                                       op1=ALU.mult).then_inc(dt_v, 1)
                e.tensor_scalar(t(S_X), t(S_X), 0.0, None, ALU.max).then_inc(dt_v, 1)
            if part < 4:
                return
            e.wait_ge(dt_v, done + 2)
            e.scalar_tensor_tensor(out=t(S_DT), in0=t(S_P), scalar=2.0, in1=t(S_X), op0=ALU.mult,
                                   op1=ALU.add).then_inc(dt_v, 1)
            e.wait_ge(dt_v, done + 3)
            e.wait_ge(dt_a, 1)
            e.tensor_scalar(t(S_DA), t(S_DT), negA[:, 0:1], -1.0, ALU.mult, ALU.mult).then_inc(dt_v, 1)
            e.wait_ge(dt_v, done + 4)
            for t0, q in CH:
                e.tensor_tensor_scan(dt_tmp[:, S_ACS, t0:t0 + q], dt_tmp[:, S_DA, t0:t0 + q],
                                     par[0:HEADS, C_ZERO:C_ZERO + 1].broadcast_to((HEADS, q)), 0.0,
                                     ALU.add, ALU.add).then_inc(dt_v, 1)
            assert done + 4 + NC == DT_STEPS

        def dt_exp_act(e):
            e.wait_ge(dt_v, 1)
            e.activation(dt_tmp[:, S_E, :], dt_tmp[:, S_E, :], ACT.Exp).then_inc(dt_a, 1)

        def dt_tables_act(e):
            e.wait_ge(dt_v, DT_STEPS)
            for t0, q in CH:
                e.activation(dt_tmp[:, S_DEC, t0:t0 + q], dt_tmp[:, S_ACS, t0:t0 + q], ACT.Exp, scale=-1.0,
                             bias=dt_tmp[:, S_ACS, t0 + q - 1:t0 + q]).then_inc(dt_a, 1)
            e.activation(dt_tmp[:, S_EXP, :], dt_tmp[:, S_ACS, :], ACT.Exp).then_inc(dt_a, 1)
            e.dma_start(scr[0], dt_tmp[:, S_ACS, :]).then_inc(scr_out, 16)
            e.wait_ge(dt_a, 8)
            e.dma_start(scr[1], dt_tmp[:, S_EXP, :]).then_inc(scr_out, 16)

        def pool_step(e, k, kp, units, ssd, fin):
            g, gp = k + -1, 1 - kp
            if ssd:
                if k.rate == 0 and k.first == 1:
                    e.wait_ge(tok_ready, 1)
                e.tensor_copy(decg[:, gp], tok[:, :, 2, at(g.mul(HPG), HPG)]).then_inc(decg_done, 1)
            for j in range(6):
                if fin and j == (1 if k.first == 9 else 2):
                    e.wait_ge(f_sq, (k + -2).mul(1, 1))
                    e.tensor_tensor(sqt[:, 0, :], sqt[:, 0, :], sqt[:, 1, :], ALU.add).then_inc(f_sum, 1)
                if ssd and j < NC:
                    q, b = CH[j][1], (gp + j) % 2
                    e.wait_ge(decg_done, g.mul(1, 1))
                    if later(g.mul(NC, j - 1)):
                        e.wait_ge(scan_done, g.mul(NC, j - 1))
                    e.wait_ge(xdt_done, g.mul(NC, j + 1))
                    e.tensor_tensor(xst[0:q, b, :].rearrange("p (r c) -> p r c", r=HPG),
                                    xdt[0:q, b, :].rearrange("p (r c) -> p r c", r=HPG),
                                    decg[0:q, gp, j, :].unsqueeze(2).broadcast_to((q, HPG, 64)),
                                    ALU.mult).then_inc(xst_done, 1)
                if ssd and 1 <= j < NC:
                    q, b = CH[j][1], (gp + j) % 2
                    decay_in(e, g, j, b)
                    e.wait_ge(conv_ready, g.mul(4, 4))
                    e.tensor_tensor(Cs[:, b, :, 0:q], bc[:, b, 1, :, 0:q],
                                    cv[:, gp, 0, CH[j][0]:CH[j][0] + q].unsqueeze(1).broadcast_to((P, HPG, q)),
                                    ALU.mult).then_inc(cs_done, 1)
                if fin and j == 2 and k.first < 9:
                    on_diagonal(e, f_rc, f_diag, k + -2)
                if units == "in":
                    look_ahead(e, split_lo, u_in(k, j))
                elif out1(k, j) is not None:
                    look_ahead(e, split_lo, Idx(U_OUT1 + out1(k, j)))

        def dve_pair(e, u, n, i, slot, ff):
            tot = i + FT * ff
            e.wait_ge(unit_done, (u + 1).v)
            free(e.tensor_tensor(halves(gb[:, slot, :]), acc_of(n), halves(rb[:]), ALU.mult), n)
            e.wait_ge(unit_done, (u + 2).v)
            free(e.tensor_tensor(halves(vb[:, slot, :]), acc_of(n + 1), halves(rb[:]), ALU.mult), n + 1)
            e.wait_ge(silu_done, (tot + 1).v)
            taken(e, n + 1)
            e.tensor_tensor(vb[:, slot, :], vb[:, slot, :], gb[:, slot, :], ALU.mult).then_inc(hid_done, 1)
            e.wait_ge(hid_hi, (tot + 1).v)
            row = hl[:, at(i.v), :].rearrange("p a t -> p (a t)")
            e.tensor_tensor(row, vb[:, slot, :], hh[:, at(i.v), :].rearrange("p a t -> p (a t)").bitcast(F32),
                            ALU.subtract).then_inc(hid_lo, 1)

        def act_pair(e, u, n, i, slot, ff):
            tot = i + FT * ff
            taken(e, n)
            e.activation(gb[:, slot, :], gb[:, slot, :], ACT.Silu).then_inc(silu_done, 1)
            look_ahead(e, split_hi, u)
            look_ahead(e, split_hi, u + 1)
            e.wait_ge(hid_done, (tot + 1).v)
            e.activation(hh[:, at(i.v), :].rearrange("p a t -> p (a t)"), vb[:, slot, :],
                         ACT.Copy).then_inc(hid_hi, 1)

        def pe_ffn(e, u0, n0, u1, n1, ff, i):
            multiply(e, Idx(u0), Idx(n0), uh, ul, moving=(u_lo, KT * i))
            multiply(e, Idx(u0 + 1), Idx(n0 + 1), uh, ul, slices=range(0, 2))
            norm_stats_pe(e, i)
            multiply(e, Idx(u0 + 1), Idx(n0 + 1), uh, ul, slices=range(2, 6))
            norm_spread_pe(e, i)
            multiply(e, Idx(u0 + 1), Idx(n0 + 1), uh, ul, slices=range(6, KT))

            def pair(e, du, t, slot):
                multiply(e, du + u0, du + n0, uh, ul)
                multiply(e, du + (u0 + 1), du + (n0 + 1), uh, ul)

            pair_turns(e, pair)

            def tile(e, du, m, slot):
                for t, ks in enumerate((KT, KT, FT - 2 * KT)):
                    e.wait_ge(hid_lo, FT * ff + KT * t + ks)
                    multiply(e, du + (u1 + t), m + n1, hh, hl, k0=KT * t, ks=ks, first=(t == 0), last=(t == 2))

            down_turns(e, tile)

        def act_ffn(e, u0, n0, u1, n1, ff, i, w):
            norm_act(e, i)
            act_pair(e, Idx(u0), Idx(n0), Idx(0), 0, ff)
            pair_turns(e, lambda e, du, t, slot: act_pair(e, du + u0, du + n0, t, slot, ff))

            def tile(e, du, m, slot):
                for t in range(3):
                    look_ahead(e, split_hi, du + (u1 + t))
                residual_act(e, m + n1, m, slot, i + 1, w)

            def between(e):
                e.activation(sd[0:RW, NR + ff:NR + ff + 1], par[0:RW, C_EPS:C_EPS + 1], ACT.Sqrt)
                if ff:
                    e.wait_ge(hid_lo, 2 * FT)
                    for k in range(POOLED):
                        e.activation(gb[:, k, :], h[:, k, :], ACT.Identity,
                                     scale=par[:, C_NORM + 40 + k:C_NORM + 41 + k]).then_inc(hw_done, 1)

            down_turns(e, tile, between)

        def dve_ffn(e, u0, n0, u1, n1, ff, i, w):
            norm_dve(e, i)
            e.wait_ge(n_rb, i + 1)
            e.wait_ge(ssq_zero, i + 1)
            dve_pair(e, Idx(u0), Idx(n0), Idx(0), 0, ff)
            pair_turns(e, lambda e, du, t, slot: dve_pair(e, du + u0, du + n0, t, slot, ff))

            def tile(e, du, m, slot):
                residual_dve(e, m + n1, (unit_done, (du + (u1 + 3)).v), m, slot, i + 1, w, h)

            down_turns(e, tile)

        def pool_ffn(e, u0, u1):
            for t in range(2):
                look_ahead(e, split_lo, Idx(u0 + t))

            def pair(e, du, t, slot):
                look_ahead(e, split_lo, du + u0)
                look_ahead(e, split_lo, du + (u0 + 1))

            def tile(e, du, m, slot):
                for t in range(3):
                    look_ahead(e, split_lo, du + (u1 + t))

            pair_turns(e, pair)
            down_turns(e, tile)

        BLOCKS = [4, 3, 2, 1, 0]
        ORDER = [("s", 0, 0), ("x", 0, 0, 2), ("fq",), ("s", 0, 1), ("vt",), ("x", 0, 2, 4), ("fs",), ("c", 0),
                 ("s", 1, 0), ("s", 1, 1), ("x", 0, 4, 6), ("fd",), ("t", 0), ("x", 0, 6, 8), ("end", 0), ("o", 0),
                 ("fb",), ("c", 1), ("x", 1, 0, 2), ("s", 2, 0), ("s", 2, 1), ("x", 1, 2, 3), ("t", 1),
                 ("x", 1, 3, 4), ("fw",), ("o", 1), ("c", 2), ("s", 3, 0), ("s", 3, 1), ("x", 1, 4, 6), ("t", 2),
                 ("x", 1, 6, 8), ("end", 1), ("o", 2), ("c", 3), ("s", 4, 0), ("s", 4, 1), ("x", 2, 0, 2),
                 ("t", 3), ("fl",), ("x", 2, 2, 4), ("o", 3), ("c", 4), ("x", 2, 4, 6), ("t", 4), ("x", 2, 6, 8),
                 ("end", 2), ("o", 4)]
        FB_AFTER = 2

        def att_steps(e, step, first):
            first(e)
            step(e, Idx(1), 1, True, True, False)
            with e.Fori(0, 3) as i:
                step(e, Idx(2, 2, i), 0, True, True, True)
                step(e, Idx(3, 2, i), 1, True, True, True)
            step(e, Idx(8), 0, False, True, True)
            step(e, Idx(9), 1, False, False, True)

        def u_att(k, j):
            return k.times(3, U_KVQ + j)

        def n_att(k, j):
            return k.times(3, N_KVQ + j)

        def early_slices(k, ev):
            _, j, a, b = ev
            if k.first == 8:
                return range(3 * (8 * j + a) // 2, 3 * (8 * j + b) // 2)
            return range(36 + (8 * j + a) // 2, 36 + (8 * j + b) // 2)

        def early_done(k, ev):
            return [s // EARLY for s in early_slices(k, ev) if s % EARLY == EARLY - 1]

        def scores(e, out, i, gp, rows, q0, k0, n):
            if i >= SPLIT_BLOCKS:
                return e.matmul(out, qT[rows, gp, q0:q0 + P], kT[rows, gp, k0:k0 + n], start=True, stop=True)
            for x, (qt, kt) in enumerate(((qTh, kTh), (qTh, kTl), (qTl, kTh))):
                mm = e.matmul(out, qt[rows, gp, q0:q0 + P], kt[rows, gp, k0:k0 + n], start=(x == 0), stop=(x == 2))
            return mm

        def pe_att(e, k, kp, units, att, fin):
            g, gp, f = k + -1, 1 - kp, k + -2
            for ev in ORDER:
                what = ev[0]
                if what == "x" and units:
                    j = ev[1]
                    multiply(e, u_att(k, j), n_att(k, j), kh if j else uh, kl if j else ul,
                             slices=range(ev[2], ev[3]))
                elif what == "x":
                    for s in early_slices(k, ev):
                        m = s // EARLY
                        if s == 0:
                            e.wait_ge(h_lo, EARLY)
                        multiply(e, Idx(U_O1 + m), Idx(N_O1 + m), oTh, oTl, ks=EARLY,
                                 slices=range(s % EARLY, s % EARLY + 1))
                elif what == "vt" and att:
                    taken(e, n_att(g, 2))
                    if later(g.mul(NC)):
                        e.wait_ge(p_tc, g.mul(NC))
                    if later(g.mul(NC)):
                        e.wait_ge(o_out, g.mul(NC))
                    for c in range(1, NC):
                        t0, q = CH[c]
                        e.transpose(psS[0:q, P * (c - 1):P * c], vT[:, t0:t0 + q], ident)
                    e.transpose(psF[0:META, P:2 * P], vT[:, 0:META], ident).then_inc(v_t, 1)
                elif what == "s" and att:
                    _, i, c = ev
                    t0, q = CH[BLOCKS[i]]
                    rows = slice(64 * c, 64 * c + 64)
                    if i == 0:
                        if c == 0:
                            taken(e, n_att(g, 0))
                            taken(e, n_att(g, 1))
                            e.wait_ge(qk_lo, g.mul(2, 2))
                        if later(g.mul(2 * NC, c)):
                            e.wait_ge(s_max, g.mul(2 * NC, c))
                        for half in range(2):
                            mm = scores(e, psAY[:, half, 0:H2], i, gp, rows, t0, H2 * half, H2)
                    else:
                        if i == 1:
                            e.wait_ge(s_max, g.mul(2 * NC, 2))
                        else:
                            e.wait_ge(s_max, g.mul(2 * NC, 2 * i + c - 1))
                        if i == FB_AFTER and c == 0 and fin:
                            e.wait_ge(h_rb, f.mul(1, 1))
                        mm = scores(e, psAY[:, c, 0:t0 + q], i, gp, rows, t0, 0, t0 + q)
                    mm.then_inc(s_mm, 1)
                elif what == "t" and att:
                    i, b = ev[1], BLOCKS[ev[1]]
                    s = (gp + i) % 2
                    e.wait_ge(p_comb, g.mul(NC, i + 1))
                    if later(g.mul(NC, i)):
                        e.wait_ge(p_tc, g.mul(NC, i))
                    if later(g.mul(NC, i)):
                        e.wait_ge(o_out, g.mul(NC, i))
                    if i == 0:
                        e.wait_ge(v_tok, g.mul(1, 1))
                    if i == 0 and fin:
                        e.wait_ge(h_sd, f.mul(1, 1))
                    for c in range(1, b + 1):
                        e.transpose(psS[:, P * (c - 1):P * c], pr[:, s, 0, CH[c][0]:CH[c][0] + P], ident)
                    e.transpose(psF[0:META, P:2 * P], pr[:, s, 0, 0:META], ident).then_inc(p_t, 1)
                elif what == "o" and att:
                    i, b = ev[1], BLOCKS[ev[1]]
                    q, s = CH[b][1], (gp + i) % 2
                    e.wait_ge(p_tc, g.mul(NC, i + 1))
                    for c in range(b + 1):
                        n = CH[c][1]
                        mm = e.matmul(psF[:, 0:q], vtok[0:n, c, :], aT[0:n, s, c, 0:q], start=(c == 0), stop=(c == b))
                    mm.then_inc(o_mm, 1)
                elif what == "fs" and fin:
                    e.wait_ge(h_sq, f.mul(1, 1))
                    if att:
                        e.wait_ge(v_tok, g.mul(1, 1))
                    else:
                        e.wait_ge(o_out, NC * AH)
                    stats(e, sqt[:, 0:1, :], 1, 2 * P).then_inc(h_stat, 1)
                elif what == "fb" and fin:
                    e.wait_ge(h_diag, f.mul(1, 1))
                    e.wait_ge(s_max, g.mul(2 * NC, 2 * FB_AFTER if att else 0))
                    spread(e, 0, psA)
                    spread(e, 1, psY).then_inc(h_bc, 1)

        def pe_att_first(e):
            multiply(e, Idx(U_KVQ), Idx(N_KVQ), uh, ul, moving=(u_lo, 2 * KT))
            multiply(e, Idx(U_KVQ + 1), Idx(N_KVQ + 1), kh, kl, slices=range(0, 2), moving=(k_lo, 0))
            norm_stats_pe(e, 2)
            multiply(e, Idx(U_KVQ + 1), Idx(N_KVQ + 1), kh, kl, slices=range(2, 6), moving=(k_lo, 0))
            norm_spread_pe(e, 2)
            multiply(e, Idx(U_KVQ + 1), Idx(N_KVQ + 1), kh, kl, slices=range(6, KT), moving=(k_lo, 0))
            multiply(e, Idx(U_KVQ + 2), Idx(N_KVQ + 2), kh, kl)

        def pe_o2(e):
            e.wait_ge(h_lo, AH)
            for m in range(KT):
                n, u = Idx(N_O2 + m), Idx(U_O2 + m // 4)
                s, a = u.first % 3, acc[n.first % 2]
                e.wait_ge(lo_ready, u.first + 1)
                if later(n.div(2).v):
                    e.wait_ge(acc_free[n.first % 2], n.div(2).v)
                for c in range(AH - EARLY):
                    k = 2 * (m % 4) + c
                    for i, (wt, mv) in enumerate(((wh, oTh), (wh, oTl), (wl, oTh))):
                        for half in range(2):
                            mm = e.matmul(a[:, half, 0:H2], wt[s][:, k, :],
                                          mv[:, EARLY + c, H2 * half:H2 * half + H2],
                                          start=(c == 0 and i == 0), stop=(c == 1 and i == 2))
                mm.then_inc(unit_done if m % 4 == 3 else o2_mm, 1)

        def o2_done(m):
            return (unit_done, U_O2 + m // 4 + 1) if m % 4 == 3 else (o2_mm, m - m // 4 + 1)

        def load_bias(e, g, gp):
            if later((g + -1).mul(2 * NC)):
                e.wait_ge(s_max, (g + -1).mul(2 * NC))
            e.dma_start(bias[:, gp, :], skewed(g)).then_inc(bias_in[gp], 16)

        def skewed(g):
            row = scr_b[at(g.v), :]
            return bass.AP(row.tensor, row.offset + P - 1, [[ND - 1, P], [1, T]])

        def act_att(e, k, kp, units, att, fin):
            g, gp, f, fp = k + -1, 1 - kp, k + -2, kp
            for ev in ORDER:
                what = ev[0]
                if what == "fq" and fin:
                    e.wait_ge(o_out, f.mul(NC, NC))
                    e.activation(sqt[:, 0, :], oraw[:, fp, :], ACT.Square).then_inc(h_sq, 1)
                elif what == "end" and units:
                    look_ahead(e, split_hi, u_att(k, ev[1]))
                    if ev[1] < 2:
                        qk_round(e, k, kp, ev[1])
                    if ev[1] == 0:
                        load_bias(e, k, kp)
                elif what == "x" and not units:
                    for m in early_done(k, ev):
                        look_ahead(e, split_hi, Idx(U_O1 + m))
                elif what == "s" and att:
                    _, i, c = ev
                    s, n = (gp + i) % 2, sum(CH[BLOCKS[i]])
                    e.wait_ge(s_max, g.mul(2 * NC, 2 * i + c + 1))
                    e.activation(pr[:, s, c, 0:n], pr[:, s, c, 0:n], ACT.Exp, scale=-1.0,
                                 bias=sm[:, s, c:c + 1], accum_out=sm[:, s, 2 + c:3 + c]).then_inc(p_exp, 1)
                elif what == "t" and att:
                    i, b = ev[1], BLOCKS[ev[1]]
                    q, s = CH[b][1], (gp + i) % 2
                    e.wait_ge(p_t, g.mul(NC, i + 1))
                    if later(g.mul(NC, i - 1)):
                        e.wait_ge(o_mm, g.mul(NC, i - 1))
                    if b:
                        e.activation(aT[:, s, 1:b + 1, :], psS[:, 0:P * b].rearrange("p (c t) -> p c t", c=b), ACT.Copy)
                    e.activation(aT[0:META, s, 0, 0:q], psF[0:META, P:P + q], ACT.Copy).then_inc(p_tc, 1)
                elif what == "fs" and fin:
                    e.wait_ge(h_stat, f.mul(1, 1))
                    e.activation(sd[0:RW, 0:NR], psF[0:RW, 2 * P:2 * P + NR], ACT.Sqrt, scale=1.0 / P,
                                 bias=par[0:RW, C_EPS:C_EPS + 1]).then_inc(h_sd, 1)
                elif what == "fb" and fin:
                    e.wait_ge(h_bc, f.mul(1, 1))
                    e.activation(halves(rb2[:]), psAY[:, :, 0:H2], ACT.Copy).then_inc(h_rb, 1)
                elif what == "fw" and fin:
                    e.wait_ge(h_on, f.mul(1, 1))
                    e.activation(oTh[:, at(f.v), :].rearrange("p a t -> p (a t)"), on[:], ACT.Copy).then_inc(h_hi, 1)

        def act_att_first(e):
            e.wait_ge(unit_done, U_KVQ)
            for k in range(KT):
                e.activation(kh[:, k, :], h[:, k, :], ACT.Identity,
                             scale=par[:, C_NORM + 16 + k:C_NORM + 17 + k]).then_inc(k_hi, 1)
            norm_act(e, 2)
            e.wait_ge(gvec_out, 16)
            load_bias(e, Idx(0), 0)
            for j in range(3):
                look_ahead(e, split_hi, Idx(U_KVQ + j))
                if j < 2:
                    qk_round(e, Idx(0), 0, j)

        def qk_round(e, k, kp, j):
            taken(e, n_att(k, j))
            if later((k + -1).mul(2 * NC)):
                e.wait_ge(s_mm, (k + -1).mul(2 * NC))
            e.activation((qTh, kTh)[j][:, kp, :], (qT, kT)[j][:, kp, :], ACT.Copy).then_inc(qk_hi, 1)

        def qk_rest(e, k, kp, j):
            e.wait_ge(qk_hi, k.mul(2, j + 1))
            e.tensor_tensor((qTl, kTl)[j][:, kp, :], (qT, kT)[j][:, kp, :], (qTh, kTh)[j][:, kp, :].bitcast(F32),
                            ALU.subtract).then_inc(qk_lo, 1)

        def dve_att(e, k, kp, units, att, fin):
            g, gp, f, fp = k + -1, 1 - kp, k + -2, kp
            for ev in ORDER:
                what = ev[0]
                if what == "end" and units:
                    take_qkv(e, k, kp, ev[1])
                elif what == "x" and not units:
                    for m in early_done(k, ev):
                        n = Idx(N_O1 + m)
                        e.wait_ge(unit_done, U_O1 + m + 1)
                        free(e.tensor_tensor(halves(h[:, m, :]), acc_of(n), halves(h[:, m, :]), ALU.add), n)
                elif what == "vt" and att:
                    e.wait_ge(v_t, g.mul(1, 1))
                    e.tensor_copy(vtok[0:META, 0, :], psF[0:META, P:2 * P])
                    e.tensor_copy(vtok[:, 1:NC, :], psS[:].rearrange("p (c t) -> p c t", c=NC - 1)).then_inc(v_tok, 1)
                elif what == "s" and att:
                    _, i, c = ev
                    t0 = CH[BLOCKS[i]][0]
                    s, n = (gp + i) % 2, sum(CH[BLOCKS[i]])
                    if i == 0 and c == 0:
                        e.wait_ge(bias_in[gp], g.div(2).mul(16, 16))
                    if later(g.mul(NC, i - 1)):
                        e.wait_ge(p_t, g.mul(NC, i - 1))
                    e.wait_ge(s_mm, g.mul(2 * NC, 2 * i + c + 1))
                    e.memset(sm[:, s, 7 + c:8 + c], 0.0)
                    src = bias[:, gp, T - P - t0:T - P - t0 + n]
                    if i:
                        io = pr[:, s, c, 0:n], psAY[:, c, 0:n], src
                    else:
                        io = halves(pr[:, s, c, :]), psAY[:, :, 0:H2], halves(src)
                    e.tensor_tensor_reduce(*io, 1.0, 3e38, ALU.add, ALU.min,
                                           sm[:, s, c:c + 1]).then_inc(s_max, 1)
                elif what == "c" and att:
                    i = ev[1]
                    s, n, done = (gp + i) % 2, sum(CH[BLOCKS[i]]), g.mul(NC, i + 1)
                    e.wait_ge(p_exp, g.mul(2 * NC, 2 * i + 2))
                    e.reciprocal(sm[:, s, 4:6], sm[:, s, 2:4]).then_inc(p_rec, 1)
                    e.wait_ge(p_rec, done)
                    e.tensor_scalar(sm[:, s, 6:7], sm[:, s, 5:6], lam[:, 5:6], None, ALU.mult).then_inc(p_lam, 1)
                    e.tensor_scalar(pr[:, s, 0, 0:n], pr[:, s, 0, 0:n], sm[:, s, 4:5], None,
                                    ALU.mult).then_inc(p_half, 1)
                    e.wait_ge(p_lam, done)
                    e.wait_ge(p_half, done)
                    e.scalar_tensor_tensor(out=pr[:, s, 0, 0:n], in0=pr[:, s, 1, 0:n], scalar=sm[:, s, 6:7],
                                           in1=pr[:, s, 0, 0:n], op0=ALU.mult, op1=ALU.add).then_inc(p_comb, 1)
                elif what == "o" and att:
                    t0, q = CH[BLOCKS[ev[1]]]
                    e.wait_ge(o_mm, g.mul(NC, ev[1] + 1))
                    e.tensor_copy(oraw[:, gp, t0:t0 + q], psF[:, 0:q]).then_inc(o_out, 1)
                elif what == "fd" and fin:
                    reciprocals(e, h_sd, h_rc, f)
                    if k.first == 9:
                        on_diagonal(e, h_rc, h_diag, f)
                elif what == "fw" and fin:
                    e.wait_ge(h_rb, f.mul(1, 1))
                    e.scalar_tensor_tensor(out=on[:], in0=oraw[:, fp, :], scalar=lam[:, 6:7], in1=rb2[:],
                                           op0=ALU.mult, op1=ALU.mult).then_inc(h_on, 1)
                elif what == "fl" and fin:
                    e.wait_ge(h_hi, f.mul(1, 1))
                    e.tensor_tensor(oTl[:, at(f.v), :].rearrange("p a t -> p (a t)"), on[:],
                                    oTh[:, at(f.v), :].rearrange("p a t -> p (a t)").bitcast(F32),
                                    ALU.subtract).then_inc(h_lo, 1)

        def take_qkv(e, k, kp, j):
            n = n_att(k, j)
            e.wait_ge(unit_done, (u_att(k, j) + 1).v)
            if j == 0:
                free(e.scalar_tensor_tensor(out=halves(qT[:, kp, :]), in0=acc_of(n), scalar=-(64 ** -0.5),
                                            in1=halves(rb[:]), op0=ALU.mult, op1=ALU.mult), n)
            else:
                dst = kT[:, kp, :] if j == 1 else vT[:]
                free(e.tensor_tensor(halves(dst), acc_of(n), halves(rb[:]), ALU.mult), n)

        def dve_att_first(e):
            for k in range(KT):
                e.wait_ge(k_hi, k + 1)
                e.scalar_tensor_tensor(out=kl[:, k, :], in0=h[:, k, :], scalar=par[:, C_NORM + 16 + k:C_NORM + 17 + k],
                                       in1=kh[:, k, :].bitcast(F32), op0=ALU.mult, op1=ALU.subtract).then_inc(k_lo, 1)
            norm_dve(e, 2)
            e.wait_ge(n_rb, 3)
            e.wait_ge(ssq_zero, 4)
            for j in range(3):
                take_qkv(e, Idx(0), 0, j)

        def pool_att(e, k, kp, units, att, fin):
            for ev in ORDER:
                if ev[0] == "fd" and fin and k.first < 9:
                    on_diagonal(e, h_rc, h_diag, k + -2)
                elif ev[0] == "end" and units:
                    look_ahead(e, split_lo, u_att(k, ev[1]))
                    if ev[1] < 2:
                        qk_rest(e, k, kp, ev[1])
                elif ev[0] == "x" and not units:
                    for m in early_done(k, ev):
                        look_ahead(e, split_lo, Idx(U_O1 + m))

        def pool_att_first(e):
            for j in range(3):
                look_ahead(e, split_lo, Idx(U_KVQ + j))
                if j < 2:
                    qk_rest(e, Idx(0), 0, j)

        @block.tensor
        def _(pe):
            multiply(pe, Idx(0), Idx(0), uh, ul, moving=(u_lo, 0))
            pe.wait_ge(con_in, 16)
            norm_stats_pe(pe, 0)
            multiply(pe, Idx(1), Idx(1), uh, ul, slices=range(0, 4))
            pe.wait_ge(ones_done, 1)
            norm_spread_pe(pe, 0)
            multiply(pe, Idx(1), Idx(1), uh, ul, slices=range(4, KT))
            pe.wait_ge(setup, 1)
            pe.matmul(psS[:, 0:2], ones[0:64, :], lam[0:64, 0:2], start=True, stop=True).then_inc(lam_mm, 1)
            pe.wait_ge(cong_in, 16)
            pe.wait_ge(n_rb, 1)
            pe.matmul(psA[0:AH, 0:512], par[0:BUCKETS, C_REL:C_REL + AH], cong[:, 0:512], start=True, stop=True)
            pe.matmul(psY[0:AH, 0:ND - 512], par[0:BUCKETS, C_REL:C_REL + AH], cong[:, 512:ND],
                      start=True, stop=True).then_inc(hot_mm, 1)
            ssd_steps(pe, pe_step)
            pe.wait_ge(f_lo, 1 + G)
            for m in range(KT):
                multiply(pe, Idx(U_OUT2 + m), Idx(N_OUT2 + m), yh[:, KT:, :], yl[:, KT:, :],
                         slices=range(6 if m < 2 else 0, KT))
            pe_ffn(pe, U_GU0, N_GU0, U_DN0, N_DN0, 0, 1)
            att_steps(pe, pe_att, pe_att_first)
            pe_o2(pe)
            pe_ffn(pe, U_GU1, N_GU1, U_DN1, N_DN1, 1, 3)
            norm_stats_pe(pe, 4)
            norm_spread_pe(pe, 4)

        @block.scalar
        def _(act):
            act.wait_ge(par_in, 16)
            act.activation(negA[:, 0:1], par[0:HEADS, C_ALOG:C_ALOG + 1], ACT.Exp).then_inc(dt_a, 1)
            split_hi(act, Idx(0))
            for k in range(KT):
                act.wait_ge(x_sem[k // 2], 16)
                act.activation(uh[:, k, :], h[:, k, :], ACT.Identity,
                               scale=par[:, C_NORM + k:C_NORM + k + 1]).then_inc(u_hi, 1)
                square(act, Idx(k), k % 2, h[:, k, :])
                if k in (5, 7):
                    split_hi(act, Idx((k - 3) // 2))
            norm_act(act, 0)
            dt_exp_act(act)
            look_ahead(act, split_hi, Idx(0))

            def reload(e):
                e.wait_ge(unit_done, U_OUT1)
                e.dma_start(part[:], x_t).then_inc(part_in, 16)

            ssd_steps(act, act_step, reload)
            for m in range(KT):
                look_ahead(act, split_hi, Idx(U_OUT2 + m))
                residual_act(act, Idx(N_OUT2 + m), Idx(m), m % 2, 1, 1)
            act_ffn(act, U_GU0, N_GU0, U_DN0, N_DN0, 0, 1, 3)
            att_steps(act, act_att, act_att_first)
            for m in range(KT):
                if m % 4 == 3:
                    look_ahead(act, split_hi, Idx(U_O2 + m // 4))
                residual_act(act, Idx(N_O2 + m), Idx(m), m % 2, 3, 4)
            act_ffn(act, U_GU1, N_GU1, U_DN1, N_DN1, 1, 3, None)
            norm_act(act, 4)

        @block.vector
        def _(dve):
            dve.wait_ge(par_in, 16)
            dve.tensor_tensor(lam[0:64, 0:2], par[0:64, C_LAM:C_LAM + 2], par[0:64, C_LAM + 2:C_LAM + 4],
                              ALU.mult).then_inc(setup, 1)
            dve.tensor_scalar(par[:, C_CONV:C_SUBLN], par[:, C_CONV:C_SUBLN], 0.5, None, ALU.mult).then_inc(setup, 1)
            dve.tensor_scalar(lam[:, 6:7], par[:, C_SUBLN:C_SUBLN + 1], 1.0 - LAMBDA_INIT, None,
                              ALU.mult).then_inc(setup, 1)
            dve.memset(ssq[:], 0.0).then_inc(ssq_zero, 1)
            dve.memset(rawc[:, 0:TAPS - 1], 0.0)
            dve.memset(tok[:], 0.0).then_inc(f_lo, 1)
            dve.wait_ge(ssq_zero, 1)
            split_lo(dve, Idx(0))
            for k in range(KT):
                dve.wait_ge(u_hi, k + 1)
                dve.scalar_tensor_tensor(out=ul[:, k, :], in0=h[:, k, :], scalar=par[:, C_NORM + k:C_NORM + k + 1],
                                         in1=uh[:, k, :].bitcast(F32), op0=ALU.mult,
                                         op1=ALU.subtract).then_inc(u_lo, 1)
                add_squares(dve, Idx(k), k % 2)
            dve.wait_ge(con_in, 16)
            dve.tensor_copy(ones_r[:], ones).then_inc(ones_done, 1)
            norm_dve(dve, 0)
            dve.wait_ge(n_rb, 1)
            dt_first(dve)
            ssd_steps(dve, dve_step)
            dve.wait_ge(ssq_zero, 2)
            for m in range(KT):
                residual_dve(dve, Idx(N_OUT2 + m), (unit_done, U_OUT2 + m + 1), Idx(m), m % 2, 1, 1, part)
            dve_ffn(dve, U_GU0, N_GU0, U_DN0, N_DN0, 0, 1, 3)
            att_steps(dve, dve_att, dve_att_first)
            take_residual(dve, Idx(N_O2), o2_done(0), Idx(0), h)
            for m in range(KT):
                if m + 1 < KT:
                    take_residual(dve, Idx(N_O2 + m + 1), o2_done(m + 1), Idx(m + 1), h)
                rest_of_residual(dve, Idx(m), m % 2, 3, 4)
            dve_ffn(dve, U_GU1, N_GU1, U_DN1, N_DN1, 1, 3, None)
            norm_dve(dve, 4)
            dve.wait_ge(n_rb, 5)
            for k in range(POOLED, KT):
                dve.scalar_tensor_tensor(out=h[:, k, :], in0=h[:, k, :],
                                         scalar=par[:, C_NORM + 40 + k:C_NORM + 41 + k], in1=rb[:],
                                         op0=ALU.mult, op1=ALU.mult).then_inc(out_f, 1)

        @block.gpsimd
        def _(pool):
            for u in range(1, 3):
                split_lo(pool, Idx(u))
            look_ahead(pool, split_lo, Idx(0))
            ssd_steps(pool, pool_step)
            for m in range(KT):
                look_ahead(pool, split_lo, Idx(U_OUT2 + m))
            pool_ffn(pool, U_GU0, U_DN0)
            att_steps(pool, pool_att, pool_att_first)
            for u in range(2):
                look_ahead(pool, split_lo, Idx(U_O2 + u))
            pool_ffn(pool, U_GU1, U_DN1)
            pool.wait_ge(n_rb, 5)
            pool.wait_ge(hw_done, POOLED)
            for k in range(POOLED):
                pool.tensor_tensor(h[:, k, :], gb[:, k, :], rb[:], ALU.mult).then_inc(out_p, 1)


def buckets():
    n = np.maximum(np.array(DIST), 0)
    exact = BUCKETS // 2
    nf = np.maximum(n, 1).astype(np.float32)
    large = exact + (np.log(nf / np.float32(exact)) / np.float32(math.log(MAX_DIST / exact))
                     * np.float32(BUCKETS - exact)).astype(np.int32)
    return np.where(n < exact, n, np.minimum(large, BUCKETS - 1))


def constants():
    con = np.zeros((P, NCON), np.float32)
    con[:, K_ONES:K_ONES + P] = 1.0
    con[:, K_ID:K_ID + P] = np.eye(P)
    con[:, K_MASK:K_MASK + P] = np.triu(np.ones((P, P)))
    con[buckets(), K_HOT + np.arange(ND)] = 1.0
    con[:, K_POS:K_POS + ND] = np.where(np.array(DIST) < 0, 1e30, 0.0)
    return con


def lay_out(a):
    w = np.zeros((UNITS, P, KT, P), np.float32)

    def put(u, block):
        ks = block.shape[0] // P
        w[u, :, :ks, :block.shape[1]] = block.reshape(ks, P, block.shape[1]).transpose(1, 0, 2)

    w_in, w_out = a["ssm_in_w"][0], a["ssm_out_w"][0]
    col = lambda m, t: m[:, P * t:P * t + P]
    put(0, w_in[:, 6144:])
    for g in range(G):
        for j, t in enumerate((40 + g, 32 + g, 16 + 2 * g, 17 + 2 * g, 2 * g, 2 * g + 1)):
            put(U_IN + 6 * g + j, col(w_in, t))
    for m in range(KT):
        put(U_OUT1 + m, col(w_out[:D], m))
        put(U_OUT2 + m, col(w_out[D:], m))
    for u_gu, u_dn, layer in ((U_GU0, U_DN0, 0), (U_GU1, U_DN1, 1)):
        gu, down = a["ffn_w_gu"][layer], a["ffn_w_down"][layer]
        for i in range(FT):
            put(u_gu + 2 * i, col(gu, i))
            put(u_gu + 2 * i + 1, col(gu, FT + i))
        for m in range(KT):
            for t in range(3):
                put(u_dn + 3 * m + t, col(down[D * t:D * (t + 1)], m))
    for hd in range(AH):
        put(U_KVQ + 3 * hd, col(a["w_q"][0], hd))
        put(U_KVQ + 3 * hd + 1, col(a["w_kv"], hd))
        put(U_KVQ + 3 * hd + 2, col(a["w_kv"], AH + hd))
    w_o = a["w_o"][0]
    for m in range(KT):
        put(U_O1 + m, col(w_o[:EARLY * P], m))
        for i in range(AH - EARLY):
            w[U_O2 + m // 4, :, 2 * (m % 4) + i, :] = col(w_o[(EARLY + i) * P:(EARLY + i + 1) * P], m)

    tiles = lambda v: v.reshape(-1, P).T
    par = np.zeros((P, NPAR), np.float32)
    for i, v in enumerate((a["norm_w"][0, 0], a["norm_w"][0, 1], a["kv_norm_w"], a["norm_w"][1, 0],
                           a["norm_w"][1, 1], a["final_norm_w"])):
        par[:, C_NORM + 8 * i:C_NORM + 8 * i + 8] = tiles(v)
    par[:, C_SSMN:C_SSMN + 16] = tiles(a["ssm_norm_w"][0])
    par[:, C_DSKIP:C_DSKIP + 16] = tiles(np.repeat(a["ssm_d"][0], 64))
    cw, cb = a["ssm_conv_w"][0], a["ssm_conv_b"][0]
    for g in range(G):
        for j, t in enumerate((24 + g, 16 + g, 2 * g, 2 * g + 1)):
            c = C_CONV + (4 * g + j) * 5
            par[:, c:c + 4] = cw[:, P * t:P * t + P].T
            par[:, c + 4] = cb[P * t:P * t + P]
    par[:, C_SUBLN] = a["subln_w"][0]
    par[:HEADS, C_DTB] = a["ssm_dt_bias"][0]
    par[:HEADS, C_ALOG] = a["ssm_a_log"][0]
    for i, name in enumerate(("lam_q1", "lam_q2", "lam_k1", "lam_k2")):
        par[:64, C_LAM + i] = a[name][0]
    par[:BUCKETS, C_REL:C_REL + AH] = a["rel_bias"]
    par[:, C_EPS] = EPS
    par[:, C_EPS + 1] = 4 * EPS

    x = np.concatenate([a["meta_tokens"], a["x"][0]], axis=0)
    x_t = np.ascontiguousarray(x.T.reshape(KT, P, T).transpose(1, 0, 2))
    return {"w_all": w.reshape(UNITS, P, KT * P), "x_t": x_t, "par": par, "con": constants()}


def kernel(**inputs):
    import concourse.bacc as bacc
    from concourse.bass_utils import run_bass_kernel_spmd

    nc = bacc.Bacc("TRN2", target_bir_lowering=False, num_devices=1, dynamic_dma_scratch_size=1024)
    arrays = lay_out({k: np.asarray(v) for k, v in inputs.items()})
    args = [nc.dram_tensor(f"{n}_dram", arrays[n].shape, F32, kind="ExternalInput").ap()
            for n in ("w_all", "x_t", "par", "con")]
    out = nc.dram_tensor("out_dram", (P, KT, SEQ), F32, kind="ExternalOutput").ap()
    build(nc, *args, out)
    r = run_bass_kernel_spmd(nc, [{f"{n}_dram": v for n, v in arrays.items()}], core_ids=[0])
    got = np.asarray(r.results[0]["out_dram"])
    return np.ascontiguousarray(got.transpose(2, 1, 0).reshape(1, SEQ, D))
```
